# Optimizing a Trainium2 kernel written in Bass

```python
import jax
import jax.numpy as jnp
from jax import lax
import numpy as np

D_MODEL = 1024
BATCH = 1
SEQ = 128
DEPTH = 2
DEC_BATCH = 1
DEC_SEQ = 256
PAST_LEN = 128

GRID_W = 64
HEAD_DIM = 64
CONV_CH = D_MODEL // 4
ATT_WIDTH = D_MODEL // 2
ATT_HEADS = ATT_WIDTH // HEAD_DIM
ATT_KV_HEADS = ATT_HEADS // 4
ATT_GQ = ATT_HEADS // ATT_KV_HEADS
KV_WIDTH = ATT_KV_HEADS * HEAD_DIM
WINDOW = 128
ATT_BLOCK = 128
RW_WIDTH = D_MODEL // 4
RW_HEADS = RW_WIDTH // HEAD_DIM
W_LORA = 64
A_LORA = 64
MIX_WIDTH = CONV_CH + ATT_WIDTH + RW_WIDTH
SPLIT_POINTS = [CONV_CH, 2 * CONV_CH, 3 * CONV_CH, 3 * CONV_CH + ATT_WIDTH,
                3 * CONV_CH + ATT_WIDTH + KV_WIDTH, 3 * CONV_CH + ATT_WIDTH + 2 * KV_WIDTH]
IN_WIDTH = SPLIT_POINTS[-1] + 5 * RW_WIDTH
N_GROUPS = 4
EXP_PER_GROUP = 8
N_EXPERTS = N_GROUPS * EXP_PER_GROUP
TOP_K = 2
D_EXPERT = D_MODEL // 2
MOE_BLOCK = 128
ROPE_BASE = 10000.0
ROT_HALF = HEAD_DIM // 2
NORM_EPS = 1e-6
GN_EPS = 64e-5
DECAY_SCALE = 0.6065306597126334
NEG_INF = -1e30

kernel_name = 'hybrid_dit_conv_swa_rwkv7_hmoe_step'

def rms_norm(x, g):
    xf = x.astype(jnp.float32)
    y = xf * lax.rsqrt(jnp.mean(xf * xf, axis=-1, keepdims=True) + NORM_EPS)
    return (y * g.astype(jnp.float32)).astype(x.dtype)

def axial_rope(x):
    n_tok = x.shape[1]
    n_rows = n_tok // GRID_W
    rows = jnp.repeat(jnp.arange(n_rows, dtype=jnp.float32), GRID_W)
    cols = (jnp.arange(n_tok) % GRID_W).astype(jnp.float32)
    inv = ROPE_BASE ** (-jnp.arange(0, ROT_HALF, 2, dtype=jnp.float32) / ROT_HALF)

    def rot(xh, pos):
        ang = pos[:, None] * inv[None, :]
        cos = jnp.cos(ang)[None, :, None, :]
        sin = jnp.sin(ang)[None, :, None, :]
        x1, x2 = xh[..., :ROT_HALF // 2], xh[..., ROT_HALF // 2:]
        return jnp.concatenate([x1 * cos - x2 * sin, x2 * cos + x1 * sin], axis=-1)

    xf = x.astype(jnp.float32)
    out = jnp.concatenate([rot(xf[..., :ROT_HALF], rows), rot(xf[..., ROT_HALF:], cols)], axis=-1)
    return out.astype(x.dtype)

def sink_softmax(scores, sink):
    s_sink = jnp.broadcast_to(sink.astype(jnp.float32).reshape(ATT_KV_HEADS, ATT_GQ, 1, 1),
                              scores.shape[:-1] + (1,))
    p = jax.nn.softmax(jnp.concatenate([scores, s_sink], axis=-1), axis=-1)
    return p[..., :-1]

def context_attention(q, k, v, sink):
    bsz, n_ctx = q.shape[:2]
    nq = n_ctx // ATT_BLOCK
    scale = HEAD_DIM ** -0.5
    qb = jnp.moveaxis(q.reshape(bsz, nq, ATT_BLOCK, ATT_KV_HEADS, ATT_GQ, HEAD_DIM), 1, 0)

    def one_block(q_blk):
        s = jnp.einsum('bqhgd,bchd->bhgqc', q_blk, k).astype(jnp.float32) * scale
        p = sink_softmax(s, sink).astype(v.dtype)
        return jnp.einsum('bhgqc,bchd->bqhgd', p, v)

    o = lax.map(one_block, qb)
    return jnp.moveaxis(o, 0, 1).reshape(bsz, n_ctx, ATT_WIDTH)

def latent_window_attention(q, k, v, k_ctx, v_ctx, sink):
    bsz, n_tok = q.shape[:2]
    nb = n_tok // ATT_BLOCK
    scale = HEAD_DIM ** -0.5
    qb = q.reshape(bsz, nb, ATT_BLOCK, ATT_KV_HEADS, ATT_GQ, HEAD_DIM)
    pad = ((0, 0), (ATT_BLOCK, ATT_BLOCK), (0, 0), (0, 0))
    kp = jnp.pad(k, pad).reshape(bsz, nb + 2, ATT_BLOCK, ATT_KV_HEADS, HEAD_DIM)
    vp = jnp.pad(v, pad).reshape(bsz, nb + 2, ATT_BLOCK, ATT_KV_HEADS, HEAD_DIM)
    k_win = jnp.concatenate([kp[:, :-2], kp[:, 1:-1], kp[:, 2:]], axis=2)
    v_win = jnp.concatenate([vp[:, :-2], vp[:, 1:-1], vp[:, 2:]], axis=2)
    s_loc = jnp.einsum('bnqhgd,bnkhd->bnhgqk', qb, k_win).astype(jnp.float32) * scale
    q_idx = jnp.arange(ATT_BLOCK)
    k_idx = jnp.arange(3 * ATT_BLOCK)
    rel = k_idx[None, :] - ATT_BLOCK - q_idx[:, None]
    k_pos = jnp.arange(nb)[:, None] * ATT_BLOCK - ATT_BLOCK + k_idx[None, :]
    valid = (jnp.abs(rel) <= WINDOW)[None] & ((k_pos >= 0) & (k_pos < n_tok))[:, None, :]
    s_loc = jnp.where(valid[None, :, None, None], s_loc, NEG_INF)
    s_ctx = jnp.einsum('bnqhgd,bchd->bnhgqc', qb, k_ctx).astype(jnp.float32) * scale
    p = sink_softmax(jnp.concatenate([s_loc, s_ctx], axis=-1), sink)
    n_loc = 3 * ATT_BLOCK
    p_loc = p[..., :n_loc].astype(v.dtype)
    p_ctx = p[..., n_loc:].astype(v.dtype)
    o = (jnp.einsum('bnhgqk,bnkhd->bnqhgd', p_loc, v_win)
         + jnp.einsum('bnhgqc,bchd->bnqhgd', p_ctx, v_ctx))
    return o.reshape(bsz, n_tok, ATT_WIDTH)

def short_conv_mixer(b_gate, c_gate, h, conv_w):
    u = c_gate * h
    up = jnp.pad(u, ((0, 0), (1, 1), (0, 0)))
    conv = up[:, :-2] * conv_w[0] + up[:, 1:-1] * conv_w[1] + up[:, 2:] * conv_w[2]
    return b_gate * conv

def wkv_scan(r, w, k, v, a, b, s0, reverse):
    def step(s, inp):
        r_t, w_t, k_t, v_t, a_t, b_t = inp
        sa = jnp.einsum('bhvk,bhk->bhv', s, a_t)
        s = (s * w_t[:, :, None, :] + sa[..., None] * b_t[:, :, None, :]
             + v_t[..., None] * k_t[:, :, None, :])
        return s, jnp.einsum('bhvk,bhk->bhv', s, r_t)

    xs = tuple(jnp.moveaxis(t, 1, 0) for t in (r, w, k, v, a, b))
    s_fin, ys = lax.scan(step, s0, xs, reverse=reverse)
    return jnp.moveaxis(ys, 0, 1), s_fin

def rwkv7_mixer(slab, mu, w0, w1, w2, a0, a1, a2, k_k, k_a, r_k, ln_g, ln_b, init_state):
    f32 = jnp.float32
    bsz, n_tok, _ = slab.shape
    hs = (bsz, n_tok, RW_HEADS, HEAD_DIM)
    xin = slab[..., :4 * RW_WIDTH]
    g = jax.nn.sigmoid(slab[..., 4 * RW_WIDTH:].astype(f32))
    y_sum = jnp.zeros(hs, f32)
    bonus = jnp.zeros(hs, f32)
    finals = []
    for d in range(2):
        if d == 0:
            nbr = jnp.pad(xin, ((0, 0), (1, 0), (0, 0)))[:, :-1]
        else:
            nbr = jnp.pad(xin, ((0, 0), (0, 1), (0, 0)))[:, 1:]
        xd = xin + (nbr - xin) * mu[d]
        r, k, v, z = jnp.split(xd, 4, axis=-1)
        w = jnp.exp(-DECAY_SCALE * jax.nn.sigmoid((w0[d] + jnp.tanh(z @ w1[d]) @ w2[d]).astype(f32)))
        a = jax.nn.sigmoid((a0[d] + (z @ a1[d]) @ a2[d]).astype(f32))
        kf = k.astype(f32)
        kk = (kf * k_k[d].astype(f32)).reshape(hs)
        kk = kk / jnp.maximum(jnp.sqrt(jnp.sum(kk * kk, axis=-1, keepdims=True)), 1e-12)
        k2 = (kf * (1.0 + (a - 1.0) * k_a[d].astype(f32))).reshape(hs)
        r_h = r.astype(f32).reshape(hs)
        v_h = v.astype(f32).reshape(hs)
        a_h = a.reshape(hs)
        if init_state is None:
            s0 = jnp.zeros((bsz, RW_HEADS, HEAD_DIM, HEAD_DIM), f32)
        else:
            s0 = init_state[:, d].astype(f32)
        y_d, s_d = wkv_scan(r_h, w.reshape(hs), k2, v_h, -kk, kk * a_h, s0, d == 1)
        y_sum = y_sum + y_d
        rk = r_k[d].astype(f32).reshape(RW_HEADS, HEAD_DIM)
        bonus = bonus + jnp.sum(r_h * k2 * rk, axis=-1, keepdims=True) * v_h
        finals.append(s_d)
    mean = jnp.mean(y_sum, axis=-1, keepdims=True)
    var = jnp.mean(jnp.square(y_sum - mean), axis=-1, keepdims=True)
    yn = ((y_sum - mean) * lax.rsqrt(var + GN_EPS)).reshape(bsz, n_tok, RW_WIDTH)
    yn = yn * ln_g.astype(f32) + ln_b.astype(f32)
    out = (yn + bonus.reshape(bsz, n_tok, RW_WIDTH)) * g
    return out.astype(slab.dtype), jnp.stack(finals, axis=1)

def grouped_expert_mlp(xf, e_idx, e_w, w1, w3, w2):
    n_tok, d = xf.shape
    n_asg = n_tok * TOP_K
    flat_e = e_idx.reshape(-1)
    order = jnp.argsort(flat_e)
    sorted_e = flat_e[order]
    counts = jnp.zeros((N_EXPERTS,), jnp.int32).at[flat_e].add(1)
    padded = (counts + MOE_BLOCK - 1) // MOE_BLOCK * MOE_BLOCK
    pad_end = jnp.cumsum(padded)
    pad_start = pad_end - padded
    start = jnp.cumsum(counts) - counts
    slot = pad_start[sorted_e] + jnp.arange(n_asg, dtype=jnp.int32) - start[sorted_e]
    n_blocks = -(-n_asg // MOE_BLOCK) + N_EXPERTS
    n_slots = n_blocks * MOE_BLOCK
    slot_tok = jnp.full((n_slots,), n_tok, jnp.int32).at[slot].set((order // TOP_K).astype(jnp.int32))
    slot_w = jnp.zeros((n_slots,), xf.dtype).at[slot].set(e_w.reshape(-1)[order])
    block_exp = jnp.minimum(
        jnp.searchsorted(pad_end, jnp.arange(n_blocks, dtype=jnp.int32) * MOE_BLOCK, side='right'),
        N_EXPERTS - 1)
    x_pad = jnp.concatenate([xf, jnp.zeros((1, d), xf.dtype)], axis=0)
    xb = x_pad[slot_tok].reshape(n_blocks, MOE_BLOCK, d)

    def expert_block(args):
        x_blk, e = args
        hid = jax.nn.silu(x_blk @ w1[e]) * (x_blk @ w3[e])
        return hid @ w2[e]

    yb = lax.map(expert_block, (xb, block_exp)).reshape(n_slots, d)
    y = jnp.zeros((n_tok + 1, d), xf.dtype).at[slot_tok].add(yb * slot_w[:, None])
    return y[:n_tok]

def hier_moe(h, rg_w, rg_b, re_w, re_b, w1, w3, w2):
    f32 = jnp.float32
    bsz, n_tok, _ = h.shape
    hf = h.reshape(-1, D_MODEL)
    n = hf.shape[0]
    g_prob = jax.nn.softmax((hf @ rg_w).astype(f32) + rg_b.astype(f32), axis=-1)
    g_top, g_idx = lax.top_k(g_prob, 1)
    e_logits = ((hf @ re_w).astype(f32) + re_b.astype(f32)).reshape(n, N_GROUPS, EXP_PER_GROUP)
    e_logits = jnp.einsum('nge,ng->ne', e_logits, jax.nn.one_hot(g_idx[:, 0], N_GROUPS, dtype=f32))
    e_prob = jax.nn.softmax(e_logits, axis=-1)
    e_top, e_loc = lax.top_k(e_prob, TOP_K)
    weights = g_top * e_top / jnp.sum(e_top, axis=-1, keepdims=True)
    idx = g_idx * EXP_PER_GROUP + e_loc
    y = grouped_expert_mlp(hf, idx, weights.astype(hf.dtype), w1, w3, w2)
    return y.reshape(bsz, n_tok, D_MODEL)

def trunk_layer(x, cond, lw, ctx_k, ctx_v, ctx_state):
    bsz, n_tok, _ = x.shape
    bc = cond.shape[0]
    mod = (jax.nn.silu(cond) @ lw['w_mod'] + lw['b_mod']).reshape(bc, 6, 1, D_MODEL)
    h = rms_norm(x, lw['norm_mix']) * (1.0 + mod[:, 1]) + mod[:, 0]
    proj = h @ lw['w_in']
    cb, cc, ch, q, k, v, rw_slab = jnp.split(proj, SPLIT_POINTS, axis=-1)
    q = q.reshape(bsz, n_tok, ATT_HEADS, HEAD_DIM)
    k = k.reshape(bsz, n_tok, ATT_KV_HEADS, HEAD_DIM)
    v = v.reshape(bsz, n_tok, ATT_KV_HEADS, HEAD_DIM)
    y_conv = short_conv_mixer(cb, cc, ch, lw['conv_w'])
    if ctx_k is None:
        y_att = context_attention(q, k, v, lw['attn_sink'])
    else:
        y_att = latent_window_attention(axial_rope(q), axial_rope(k), v, ctx_k, ctx_v, lw['attn_sink'])
    y_rw, s_fin = rwkv7_mixer(rw_slab, lw['rw_mu'], lw['rw_w0'], lw['rw_w1'], lw['rw_w2'],
                              lw['rw_a0'], lw['rw_a1'], lw['rw_a2'], lw['rw_kk'], lw['rw_ka'],
                              lw['rw_rk'], lw['rw_ln_g'], lw['rw_ln_b'], ctx_state)
    mix = jnp.concatenate([y_conv, y_att, y_rw], axis=-1) @ lw['w_out']
    x = x + mod[:, 2] * mix
    h2 = rms_norm(x, lw['norm_ffn']) * (1.0 + mod[:, 4]) + mod[:, 3]
    x = x + mod[:, 5] * hier_moe(h2, lw['rt_group_w'], lw['rt_group_b'], lw['rt_exp_w'],
                                 lw['rt_exp_b'], lw['exp_w1'], lw['exp_w3'], lw['exp_w2'])
    if ctx_k is None:
        return x, k, v, s_fin
    return x

def setup_inputs(seed: int = 0) -> dict:
    key = jax.random.key(seed)
    ks = list(jax.random.split(key, 40))
    f32 = jnp.float32
    d = D_MODEL

    def nrm(i, shape, scale):
        return jax.random.normal(ks[i], shape, f32) * scale

    return {
        'x_prompt': nrm(0, (BATCH, SEQ, d), 1.0),
        'x_sample': nrm(1, (DEC_BATCH, DEC_SEQ, d), 1.0),
        'cache_k': nrm(2, (DEC_BATCH, DEPTH, PAST_LEN, ATT_KV_HEADS, HEAD_DIM), 1.0),
        'cache_v': nrm(3, (DEC_BATCH, DEPTH, PAST_LEN, ATT_KV_HEADS, HEAD_DIM), 1.0),
        'state_wkv': nrm(4, (DEC_BATCH, DEPTH, 2, RW_HEADS, HEAD_DIM, HEAD_DIM), 0.5),
        'c': nrm(5, (DEC_BATCH, d), 1.0),
        'c_ctx': nrm(6, (d,), 1.0),
        'w_mod': nrm(7, (DEPTH, d, 6 * d), 0.5 * d ** -0.5),
        'b_mod': nrm(8, (DEPTH, 6 * d), 0.02),
        'norm_mix': 1.0 + nrm(9, (DEPTH, d), 0.05),
        'norm_ffn': 1.0 + nrm(10, (DEPTH, d), 0.05),
        'norm_out': 1.0 + nrm(11, (d,), 0.05),
        'w_in': nrm(12, (DEPTH, d, IN_WIDTH), d ** -0.5),
        'w_out': nrm(13, (DEPTH, MIX_WIDTH, d), MIX_WIDTH ** -0.5),
        'conv_w': nrm(14, (DEPTH, 3, CONV_CH), 0.5),
        'attn_sink': nrm(15, (DEPTH, ATT_HEADS), 0.5),
        'rw_mu': jax.random.uniform(ks[16], (DEPTH, 2, 4 * RW_WIDTH), f32),
        'rw_w0': nrm(17, (DEPTH, 2, RW_WIDTH), 1.0),
        'rw_w1': nrm(18, (DEPTH, 2, RW_WIDTH, W_LORA), RW_WIDTH ** -0.5),
        'rw_w2': nrm(19, (DEPTH, 2, W_LORA, RW_WIDTH), 0.5 * W_LORA ** -0.5),
        'rw_a0': nrm(20, (DEPTH, 2, RW_WIDTH), 0.5),
        'rw_a1': nrm(21, (DEPTH, 2, RW_WIDTH, A_LORA), RW_WIDTH ** -0.5),
        'rw_a2': nrm(22, (DEPTH, 2, A_LORA, RW_WIDTH), 0.5 * A_LORA ** -0.5),
        'rw_kk': 0.85 + nrm(23, (DEPTH, 2, RW_WIDTH), 0.05),
        'rw_ka': 1.0 + nrm(24, (DEPTH, 2, RW_WIDTH), 0.05),
        'rw_rk': nrm(25, (DEPTH, 2, RW_WIDTH), 0.1),
        'rw_ln_g': 1.0 + nrm(26, (DEPTH, RW_WIDTH), 0.05),
        'rw_ln_b': nrm(27, (DEPTH, RW_WIDTH), 0.01),
        'rt_group_w': nrm(28, (DEPTH, d, N_GROUPS), d ** -0.5),
        'rt_group_b': nrm(29, (DEPTH, N_GROUPS), 0.01),
        'rt_exp_w': nrm(30, (DEPTH, d, N_EXPERTS), d ** -0.5),
        'rt_exp_b': nrm(31, (DEPTH, N_EXPERTS), 0.01),
        'exp_w1': nrm(32, (DEPTH, N_EXPERTS, d, D_EXPERT), d ** -0.5),
        'exp_w3': nrm(33, (DEPTH, N_EXPERTS, d, D_EXPERT), d ** -0.5),
        'exp_w2': nrm(34, (DEPTH, N_EXPERTS, D_EXPERT, d), D_EXPERT ** -0.5),
    }

def reference(x_prompt, x_sample, cache_k, cache_v, state_wkv, c, c_ctx, w_mod, b_mod,
              norm_mix, norm_ffn, norm_out, w_in, w_out, conv_w, attn_sink, rw_mu, rw_w0,
              rw_w1, rw_w2, rw_a0, rw_a1, rw_a2, rw_kk, rw_ka, rw_rk, rw_ln_g, rw_ln_b,
              rt_group_w, rt_group_b, rt_exp_w, rt_exp_b, exp_w1, exp_w3, exp_w2):
    x_p = x_prompt
    x_s = x_sample
    cond_p = c_ctx[None, :]
    keys_p, vals_p, states_p = [], [], []
    for l in range(DEPTH):
        lw = {
            'w_mod': w_mod[l], 'b_mod': b_mod[l], 'norm_mix': norm_mix[l], 'norm_ffn': norm_ffn[l],
            'w_in': w_in[l], 'w_out': w_out[l], 'conv_w': conv_w[l], 'attn_sink': attn_sink[l],
            'rw_mu': rw_mu[l], 'rw_w0': rw_w0[l], 'rw_w1': rw_w1[l], 'rw_w2': rw_w2[l],
            'rw_a0': rw_a0[l], 'rw_a1': rw_a1[l], 'rw_a2': rw_a2[l], 'rw_kk': rw_kk[l],
            'rw_ka': rw_ka[l], 'rw_rk': rw_rk[l], 'rw_ln_g': rw_ln_g[l], 'rw_ln_b': rw_ln_b[l],
            'rt_group_w': rt_group_w[l], 'rt_group_b': rt_group_b[l], 'rt_exp_w': rt_exp_w[l],
            'rt_exp_b': rt_exp_b[l], 'exp_w1': exp_w1[l], 'exp_w3': exp_w3[l], 'exp_w2': exp_w2[l],
        }
        x_p, k_l, v_l, s_l = trunk_layer(x_p, cond_p, lw, None, None, None)
        keys_p.append(k_l)
        vals_p.append(v_l)
        states_p.append(s_l.astype(x_prompt.dtype))
        x_s = trunk_layer(x_s, c, lw, cache_k[:, l], cache_v[:, l], state_wkv[:, l])
    y_prompt = rms_norm(x_p, norm_out)
    y_sample = rms_norm(x_s, norm_out)
    new_cache_k = jnp.stack(keys_p, axis=1)
    new_cache_v = jnp.stack(vals_p, axis=1)
    new_state_wkv = jnp.stack(states_p, axis=1)
    return (y_prompt, y_sample, new_cache_k, new_cache_v, new_state_wkv)


_drawn_inputs = setup_inputs


def setup_inputs(seed=0):
    import zlib

    import numpy as np

    out = dict(_drawn_inputs(seed))
    spreads = {}
    factors = {'cache_k': 2.737,
     'state_wkv': 6.265,
     'attn_sink': 34.185,
     'rw_kk': 11.068,
     'rw_ln_g': 5.119,
     'rw_ln_b': 36.5,
     'rt_group_b': 8.0,
     'rt_exp_b': 18.309}
    for name, (base, spread) in spreads.items():
        noise = np.random.default_rng([zlib.crc32(name.encode()), seed]).standard_normal(out[name].shape)
        drawn = base * np.exp(spread * noise) if base else spread * noise
        out[name] = jnp.asarray(drawn.astype(out[name].dtype))
    for name, factor in factors.items():
        out[name] = (out[name] * factor).astype(out[name].dtype)
    return out
```

```python
import numpy as np
import concourse.bass as bass
from concourse import mybir
from contextlib import ExitStack

F32 = mybir.dt.float32
I32 = mybir.dt.int32
ACT = mybir.ActivationFunctionType
ALU = mybir.AluOpType
AX = mybir.AxisListType

P = 128
DEPTH = 2
D = 1024
KC = D // P
TP, TS = 128, 256
T = TP + TS
TILES = T // P
W = T + 3
COL = (1, 2 + TP)
HD = 64
CONV, ATT, KV, RW = 256, 512, 128, 256
IN_W = 3 * CONV + ATT + 2 * KV + 5 * RW
N_GROUPS, EPG = 4, 8
N_EXP = N_GROUPS * EPG
DE = D // 2
FC = DE // P
SLOTS = 64
MAX_ROUNDS = T // SLOTS
DECAY = 0.6065306597126334
NORM_EPS, GN_EPS = 1e-6, 64e-5
LEVELS = 7
UC = 256

PK, _n = {}, 0
for _name, _w in (("b_mod", 48), ("norm_mix", 8), ("norm_ffn", 8), ("conv_w", 6), ("mu", 16), ("w0", 4),
                  ("a0", 4), ("kk", 4), ("ka", 4), ("rk", 4), ("ln_g", 2), ("ln_b", 2), ("sink", 8), ("rt_b", 36)):
    PK[_name] = _n
    _n += _w
NPK = _n

CK, _n = {}, 0
for _name, _w in (("ident", P), ("ones", P), ("heads", P), ("before", P), ("swap", P), ("dup", 2 * P),
                  ("cos", TS), ("sin", TS), ("att", 2 * P), ("tri", 4 * P), ("level", 2 * LEVELS * P),
                  ("reset", 3 * 129), ("iota", SLOTS), ("rev", EPG), ("eps", 2)):
    CK[_name] = _n
    _n += _w
NCK = _n


def build(nc, a, o):
    ctx = ExitStack()
    with ctx:
        def sb(name, cols, dt=F32):
            return ctx.enter_context(nc.sbuf_tensor(name, [P, cols], dt))

        sems = {}

        def sem(name):
            if name not in sems:
                sems[name] = ctx.enter_context(nc.semaphore(name))
            return sems[name]

        x_sb = sb("x_sb", KC * T)
        xT = x_sb[:, :].rearrange("p (c t) -> p c t", c=KC)
        const = sb("const", NCK)
        par = sb("par", NPK)
        nout = sb("nout", KC)
        cond = sb("cond", 2 * KC)
        scond = sb("scond", 2 * KC)
        mod_sb = sb("mod_sb", 96)
        mod = mod_sb[:, :].rearrange("p (j s) -> p j s", s=2)
        gains = sb("gains", 32)
        gain = gains[:, :].rearrange("p (n c s) -> p n c s", n=2, s=2)
        posm = sb("posm", TILES * N_EXP)
        wall = sb("wall", TILES * N_EXP)
        rounds_i = sb("rounds_i", 1, I32)
        AR_N = 45168
        arena = sb("arena", AR_N)

        bank = [ctx.enter_context(nc.psum_tensor(f"bank{i}", [P, 512], F32)) for i in range(8)]

        def ck(name, n, off=0):
            return const[:, CK[name] + off:CK[name] + off + n]

        def pk(name, i=0, n=1):
            return par[:, PK[name] + i:PK[name] + i + n]

        ident, ones, heads = ck("ident", P), ck("ones", P), ck("heads", P)

        at = [0]

        def take(n):
            at[0] += n
            assert at[0] <= AR_N, at[0]
            return arena[:, at[0] - n:at[0]]

        stream = [take(KC * UC).rearrange("p (c n) -> p c n", c=KC) for _ in range(2)]
        h_at = at[0]
        hT = take(KC * W + 4)[:, 0:KC * W].rearrange("p (c w) -> p c w", c=KC)
        Pm = arena[:, h_at:h_at + 1536].rearrange("p (h k) -> p h k", h=4)
        PT = arena[:, h_at + 1536:h_at + 3072].rearrange("p (k h q) -> p k h q", k=3, h=4)
        slab = take(8 * W).rearrange("p (c w) -> p c w", c=8)
        gate = take(2 * T).rearrange("p (c t) -> p c t", c=2)
        conv_at = at[0]
        conv = take(6 * W).rearrange("p (c w) -> p c w", c=6)
        qT = take(4 * T).rearrange("p (c t) -> p c t", c=4)
        kT = take(512)
        vT = take(T)
        Kd = take(1024).rearrange("p (g k) -> p g k", g=2)
        Vt = take(4 * P).rearrange("p (t d) -> p t d", t=4)
        mix_at = at[0]
        mixT = take(KC * T).rearrange("p (c t) -> p c t", c=KC)
        kraw = mixT[:, 2, 0:TS]
        rtmp = mixT[:, 5:8, :].rearrange("p c t -> p (c t)")[:, 0:1024]
        diff = take(8 * (W - 1)).rearrange("p (c w) -> p c w", c=8)
        Z = take(2 * T).rearrange("p (c t) -> p c t", c=2)
        R_, K_, V_ = take(T), take(T), take(T)
        lora = [take(T), take(T)]
        Sg = take(3 * 129)
        Lp = take(3 * 129)
        Ep, Em = take(3 * 129), take(3 * 129)
        A_, kkn, rn, t1, t2 = take(T), take(T), take(T), take(T), take(T)
        AR = [take(3 * 256).rearrange("p (t a q) -> p t a q", t=3, a=2) for _ in range(2)]
        BT = [take(T) for _ in range(2)]
        KT = [take(T) for _ in range(2)]
        tok = [take(3 * T).rearrange("p (w t d) -> p w t d", w=3, t=3) for _ in range(2)]
        ec = take(4 * 6).rearrange("p (l w t) -> p l w t", l=4, w=2)
        bonus = take(2 * T).rearrange("p (c t) -> p c t", c=2)
        ys = take(2 * T).rearrange("p (c t) -> p c t", c=2)
        G = take(6 * 512).rearrange("p (t h w a q) -> p t h w a q", t=3, h=2, w=2, a=2)
        X_, XT = (take(6 * P).rearrange("p (i q) -> p i q", i=6) for _ in range(2))
        T1 = arena[:, conv_at:conv_at + 6 * P].rearrange("p (i q) -> p i q", i=6)
        Nl = [take(6 * P).rearrange("p (i q) -> p i q", i=6) for _ in range(2)]
        S0 = take(4 * HD).rearrange("p (l v) -> p l v", l=4)
        S0c = take(P)
        Sout = take(4 * HD).rearrange("p (l v) -> p l v", l=4)
        rhs = take(P)
        SA = take(P)
        ss, rstd = R_, K_
        stmp = take(HD)
        cmid = take(TILES)
        w1a1 = take(2 * 2 * P).rearrange("p (d k m) -> p d k m", d=2, k=2)
        w2a2 = take(2 * RW).rearrange("p (d m) -> p d m", d=2)
        rtw = take(KC * 36).rearrange("p (c e) -> p c e", c=KC)
        negmu, omka = take(8), take(4)
        mx, sums, negm, esink, rden = take(4), take(4), take(4), take(4), take(4)
        sq = mixT
        n1 = mixT
        h2T = arena[:, h_at:h_at + KC * T].rearrange("p (c t) -> p c t", c=KC)
        r_at = [h_at + KC * T + 24]

        def rt(n):
            r_at[0] += n
            return arena[:, r_at[0] - n:r_at[0]]

        lg = rt(TILES * 36).rearrange("p (t e) -> p t e", t=TILES)
        gm, gs = rt(TILES), rt(TILES)
        gx = rt(TILES * 4).rearrange("p (t g) -> p t g", t=TILES)
        goh = rt(TILES * 4).rearrange("p (t g) -> p t g", t=TILES)
        el4 = rt(TILES * N_EXP).rearrange("p (t g e) -> p t g e", t=TILES, g=N_GROUPS)
        el = rt(TILES * EPG).rearrange("p (t e) -> p t e", t=TILES)
        oh1 = rt(TILES * EPG).rearrange("p (t e) -> p t e", t=TILES)
        oh2 = rt(TILES * EPG).rearrange("p (t e) -> p t e", t=TILES)
        tw = rt(TILES * EPG).rearrange("p (t e) -> p t e", t=TILES)
        m1, m2, e21, w1_, w2_ = rt(TILES), rt(TILES), rt(TILES), rt(TILES), rt(TILES)
        asg = rt(TILES * N_EXP).rearrange("p (t g e) -> p t g e", t=TILES, g=N_GROUPS)
        rnd = rt(8)
        assert r_at[0] <= mix_at

        unit = [arena[:, i * 4096:(i + 1) * 4096] for i in range(2)]
        h2tok = arena[:, mix_at:mix_at + TILES * D].rearrange("p (t d) -> p t d", t=TILES)
        assert 2 * 4096 <= mix_at
        m_at = mix_at + TILES * D
        unit += [arena[:, m_at + i * 4096:m_at + (i + 1) * 4096] for i in range(4)]
        m_at += 4 * 4096
        e_at = [2 * 4096]

        def moe(n):
            if e_at[0] + n > mix_at and e_at[0] < m_at:
                e_at[0] = m_at
            e_at[0] += n
            assert e_at[0] <= AR_N
            return arena[:, e_at[0] - n:e_at[0]]

        Sel = moe(TILES * P).rearrange("p (t j s) -> p t j s", t=TILES, j=2)
        Wsel = moe(TILES * P).rearrange("p (t j s) -> p t j s", t=TILES, j=2)
        WselT = moe(T)
        Xg = moe(KC * P).rearrange("p (c j s) -> p c j s", c=KC, j=2)
        sil, hid = moe(DE), moe(DE)
        hidT = moe(FC * P).rearrange("p (f j s) -> p f j s", f=FC, j=2)
        yg = moe(D)

        pos3 = posm[:, :].rearrange("p (t e) -> p t e", t=TILES)
        wall3 = wall[:, :].rearrange("p (t e) -> p t e", t=TILES)

        def clear(block_sems):
            with nc.Block() as block:
                @block.sync
                def _(sp):
                    for s in block_sems:
                        sp.sem_clear(s)

        class Lane:

            def __init__(self, eng, name):
                self.eng, self.s, self.n, self.counts = eng, sem(name), 0, {}

            def step(self, ins, hold=True):
                self.n += 1
                ins.then_inc(self.s, 1)
                if hold:
                    self.eng.wait_ge(self.s, self.n)

            def sig(self, ins, name, hold=True):
                self.counts[name] = self.counts.get(name, 0) + 1
                ins.then_inc(sem(name), 1)
                if hold:
                    self.eng.wait_ge(sem(name), self.counts[name])

            def free(self, ins, turns, name, hold=True):
                ins.then_inc(sem(f"bank_emptied{turns.place[name][0]}"), 1)
                if hold:
                    turns.copied(self.eng, name)

        class PsumTurns:

            def __init__(self, banks):
                self.banks, self.n, self.count, self.place = banks, 0, {}, {}

            def open(self, pe, name):
                b = self.banks[self.n % len(self.banks)]
                self.n += 1
                if self.count.get(b):
                    pe.wait_ge(sem(f"bank_emptied{b}"), self.count[b])
                self.count[b] = self.count.get(b, 0) + 1
                self.place[name] = (b, self.count[b])
                return bank[b]

            def close(self, last, name):
                last.then_inc(sem(f"bank_filled{self.place[name][0]}"), 1)

            def filled(self, eng, name):
                b, n = self.place[name]
                eng.wait_ge(sem(f"bank_filled{b}"), n)
                return bank[b]

            def copied(self, eng, name):
                b, n = self.place[name]
                eng.wait_ge(sem(f"bank_emptied{b}"), n)

        HALF = (slice(0, HD), slice(HD, P))
        STREAMS = ((slice(0, TP), slice(1, 1 + TP)), (slice(TP, T), slice(2 + TP, 2 + T)))
        LANES = [(d, c) for d in range(2) for c in range(2)]
        TILE_ORDER = ((0, 1, 2), (0, 2, 1))
        ATT_GROUPS = [(q, g) for q in range(3) for g in range(2)]
        N_MOD, N_IN, N_OUT = 6 * D // UC, IN_W // UC, D // UC
        IN_ORDER = (6, 7, 8, 9, 10, 3, 4, 5, 0, 1, 2)

        def keys(q):
            return (0,) if q == 0 else (1, 2, 3)

        def mixer_stage(layer):
            pr = PsumTurns(list(range(8)))
            piece_free = {}

            with nc.Block() as block:
                @block.tensor
                def _(pe):
                    mm = nc.tensor.matmul

                    def piece(n):
                        pe.wait_ge(sem(f"piece_loaded{n % 2}"), 16 * (n // 2 + 1))
                        return stream[n % 2]

                    b = pr.open(pe, "mod")
                    for n in range(N_MOD):
                        w = piece(n)
                        for j in range(UC // P):
                            col = 2 * (n * UC // P + j)
                            for c in range(KC):
                                last = mm(b[:, col:col + 2], w[:, c, j * P:(j + 1) * P],
                                          scond[:, 2 * c:2 * c + 2], start=(c == 0), stop=(c == KC - 1))
                        if n < N_MOD - 1:
                            last.then_inc(sem(f"piece_used{n % 2}"), 1)
                            piece_free[n] = (f"piece_used{n % 2}", n // 2 + 1)
                    pr.close(last, "mod")
                    piece_free[N_MOD - 1] = ("bank_filled0", 1)

                    def channel_sum(name, lhsT, src, chunks):
                        b = pr.open(pe, name)
                        for n, c in enumerate(chunks):
                            last = mm(b[:, 0:T], lhsT, src[:, c, :], start=(n == 0), stop=(n == len(chunks) - 1))
                        pr.close(last, name)

                    pe.wait_ge(sem("sq_ready"), 1)
                    channel_sum("ss1", ones, sq, range(KC))

                    pe.wait_ge(sem("h_ready"), 1)
                    n = N_MOD

                    def project(pieces):
                        nonlocal n
                        for u in pieces:
                            w = piece(n)
                            for j in range(UC // P):
                                name = f"in{u * UC // P + j}"
                                b = pr.open(pe, name)
                                for c in range(KC):
                                    last = mm(b[:, 0:W - 2], w[:, c, j * P:(j + 1) * P], hT[:, c, 1:W - 1],
                                              start=(c == 0), stop=(c == KC - 1))
                                pr.close(last, name)
                            piece_free[n] = (f"bank_filled{pr.place[name][0]}", pr.place[name][1])
                            n += 1

                    project(IN_ORDER)

                    def lora1(d):
                        pe.wait_ge(sem("z_ready"), d + 1)
                        b = pr.open(pe, f"lora1_{d}")
                        for k in range(2):
                            last = mm(b[:, 0:T], w1a1[:, d, k, :], Z[:, k, :], start=(k == 0), stop=(k == 1))
                        pr.close(last, f"lora1_{d}")

                    def lora2(l):
                        d, c = LANES[l]
                        if c == 0:
                            pr.copied(pe, f"lora1_{d}")
                        for half, name in enumerate(("decay", "rate")):
                            b = pr.open(pe, f"{name}{l}")
                            last = mm(b[:, 0:T], w2a2[HALF[half], d, c * P:(c + 1) * P], lora[d][HALF[half], :],
                                      start=True, stop=True)
                            pr.close(last, f"{name}{l}")

                    def head_sum(name, src, ready, count):
                        pe.wait_ge(sem(ready), count)
                        b = pr.open(pe, name)
                        pr.close(mm(b[:, 0:T], heads, src, start=True, stop=True), name)

                    def token_major(l, what, src, ready):
                        pe.wait_ge(sem(ready), l + 1)
                        b = pr.open(pe, f"{what}{l}")
                        for t in range(TILES):
                            last = nc.tensor.transpose(b[:, t * P:(t + 1) * P], src[:, t * P:(t + 1) * P], ident)
                        pr.close(last, f"{what}{l}")

                    def scores(l):
                        q = l % 2
                        pe.wait_ge(sem("decayed_ready"), l + 1)
                        for t in range(TILES):
                            for h in range(2):
                                b = pr.open(pe, f"g{l}_{t}_{h}")
                                for w, src in enumerate((BT, KT)):
                                    last = mm(b[:, w * 256:(w + 1) * 256], src[q][HALF[h], t * P:(t + 1) * P],
                                              AR[q][HALF[h], t, :, :], start=True, stop=True)
                                pr.close(last, f"g{l}_{t}_{h}")

                    def prepare(l):
                        lora2(l)
                        head_sum(f"norm{l}", t1, "ksq_ready", l + 1)
                        token_major(l, "tokv", V_, "v_ready")
                        head_sum(f"bon{l}", t2, "rk_ready", l + 1)
                        token_major(l, "tokb", BT[l % 2], "decayed_ready")
                        token_major(l, "tokk", KT[l % 2], "decayed_ready")
                        scores(l)

                    def invert(l):
                        for lev in range(LEVELS):
                            pe.wait_ge(sem("level_ready"), l * LEVELS + lev + 1)
                            for half in range(2):
                                ii = range(3 * half, 3 * half + 3)
                                if lev == 1:
                                    pe.wait_ge(sem("x_ready"), 2 * l + half + 1)
                                elif lev:
                                    pr.copied(pe, f"dxt_{l}_{lev - 1}_{half}")
                                b = pr.open(pe, f"t1_{l}_{lev}_{half}")
                                for i in ii:
                                    last = mm(b[:, (i % 3) * P:(i % 3 + 1) * P], Nl[lev % 2][:, i, :],
                                              X_[:, i, :] if lev else ident, start=True, stop=True)
                                pr.close(last, f"t1_{l}_{lev}_{half}")
                            for half in range(2):
                                ii = range(3 * half, 3 * half + 3)
                                if not lev:
                                    continue
                                pr.copied(pe, f"t1_{l}_{lev}_{half}")
                                for what in ("dx", "dxt"):
                                    if what == "dx" and lev == LEVELS - 1:
                                        continue
                                    b = pr.open(pe, f"{what}_{l}_{lev}_{half}")
                                    for i in ii:
                                        o_ = b[:, (i % 3) * P:(i % 3 + 1) * P]
                                        if what == "dx":
                                            last = mm(o_, XT[:, i, :], T1[:, i, :], start=True, stop=True)
                                        else:
                                            last = mm(o_, T1[:, i, :], XT[:, i, :], start=True, stop=True)
                                    pr.close(last, f"{what}_{l}_{lev}_{half}")

                    def solve(l):
                        d, c = LANES[l]
                        q = l % 2
                        pr.copied(pe, f"tokk{l}")
                        pr.copied(pe, f"tokb{l}")
                        pr.copied(pe, f"tokv{l}")
                        for half in range(2):
                            pr.copied(pe, f"dxt_{l}_{LEVELS - 1}_{half}")
                        for n_, t in enumerate(TILE_ORDER[d]):
                            seeded = n_ > 0
                            vtok, btok, ktok = (tok[q][:, w, t, :] for w in range(3))
                            if seeded:
                                pe.wait_ge(sem("seed_ready"), 2 * l + n_)
                            b = pr.open(pe, f"rhs{l}_{t}")
                            if seeded:
                                mm(b[:, 0:P], AR[q][:, t, 0, :], S0c, start=True, stop=True, skip_group_check=True)
                            for h in range(2):
                                last = mm(b[:, h * HD:(h + 1) * HD], G[:, t, h, 1, 0, :], vtok[:, HALF[h]],
                                          start=not seeded, stop=True, skip_group_check=True)
                            pr.close(last, f"rhs{l}_{t}")
                            pr.copied(pe, f"rhs{l}_{t}")
                            b = pr.open(pe, f"sa{l}_{t}")
                            for h in range(2):
                                last = mm(b[:, h * HD:(h + 1) * HD], XT[:, 2 * t + h, :], rhs[:, h * HD:(h + 1) * HD],
                                          start=True, stop=True)
                            pr.close(last, f"sa{l}_{t}")
                            pr.copied(pe, f"sa{l}_{t}")
                            if n_ < 2:
                                b = pr.open(pe, f"state{l}_{t}")
                                for h in range(2):
                                    mm(b[HALF[h], 0:HD], btok[:, HALF[h]], SA[:, h * HD:(h + 1) * HD],
                                       start=True, stop=False)
                                    last = mm(b[HALF[h], 0:HD], ktok[:, HALF[h]], vtok[:, HALF[h]],
                                              start=False, stop=True)
                                pr.close(last, f"state{l}_{t}")
                            b = pr.open(pe, f"y{l}_{t}")
                            if seeded:
                                mm(b[:, 0:P], S0c, AR[q][:, t, 1, :], start=True, stop=True, skip_group_check=True)
                            for h in range(2):
                                o_ = b[HALF[h], 0:P]
                                mm(o_, vtok[:, HALF[h]], G[:, t, h, 1, 1, :], start=not seeded, stop=True,
                                   skip_group_check=True)
                                last = mm(o_, SA[:, h * HD:(h + 1) * HD], G[:, t, h, 0, 1, :], start=False, stop=True,
                                          skip_group_check=True)
                            pr.close(last, f"y{l}_{t}")

                    def attention_inputs():
                        for n_ in range(3):
                            pr.copied(pe, f"in{(6, 8, 10)[n_]}")
                            pr.copied(pe, f"in{(7, 9, 11)[n_]}")
                        b = pr.open(pe, "swapk")
                        pr.close(mm(b[:, 0:TS], ck("swap", P), kraw[:, :], start=True, stop=True), "swapk")
                        for j in range(2):
                            b = pr.open(pe, f"swapq{j}")
                            for i in range(2):
                                last = mm(b[:, i * TS:(i + 1) * TS], ck("swap", P), qT[:, 2 * j + i, TP:T],
                                          start=True, stop=True)
                            pr.close(last, f"swapq{j}")
                        b = pr.open(pe, "vtok")
                        for t in range(TILES):
                            last = nc.tensor.transpose(b[:, t * P:(t + 1) * P], vT[:, t * P:(t + 1) * P], ident)
                        pr.close(last, "vtok")
                        pe.wait_ge(sem("k_roped"), 1)
                        for g in range(2):
                            b = pr.open(pe, f"kdup{g}")
                            pr.close(mm(b[:, :], ck("dup", P, g * P), kT[:, :], start=True, stop=True), f"kdup{g}")
                        pe.wait_ge(sem("q_roped"), 2)
                        pr.copied(pe, "kdup0")
                        pr.copied(pe, "kdup1")
                        pr.copied(pe, "vtok")

                    def att_scores(q, g):
                        if q == 0:
                            for par_ in range(2):
                                b = pr.open(pe, f"s{q}{g}{par_}")
                                for h in (par_, par_ + 2):
                                    head = 4 * g + h
                                    last = mm(b[:, (h // 2) * P:(h // 2 + 1) * P], qT[HALF[par_], head // 2, 0:P],
                                              Kd[HALF[par_], g, 0:P], start=True, stop=True)
                                pr.close(last, f"s{q}{g}{par_}")
                            return
                        for h in range(4):
                            head = 4 * g + h
                            rows = HALF[head % 2]
                            lhsT = qT[rows, head // 2, q * P:(q + 1) * P]
                            b = pr.open(pe, f"s{q}{g}{h}")
                            mm(b[:, 0:3 * P], lhsT, Kd[rows, g, P:4 * P], start=True, stop=True)
                            off = (2 - q) * P
                            last = mm(b[:, off:off + P], ident, ck("att", P, (q - 1) * P), start=False, stop=True,
                                      skip_group_check=True)
                            pr.close(last, f"s{q}{g}{h}")

                    def att_values(q, g):
                        n_ = ATT_GROUPS.index((q, g))
                        pe.wait_ge(sem("p_ready"), n_ + 1)
                        nk = len(keys(q))
                        for k in range(nk):
                            b = pr.open(pe, f"pt{q}{g}{k}")
                            for h in range(4):
                                last = nc.tensor.transpose(b[:, h * P:(h + 1) * P], Pm[:, h, k * P:(k + 1) * P], ident)
                            pr.close(last, f"pt{q}{g}{k}")
                        for k in range(nk):
                            pr.copied(pe, f"pt{q}{g}{k}")
                        b = pr.open(pe, f"o{q}{g}")
                        for h in range(4):
                            o_ = b[HALF[h % 2], (h // 2) * P:(h // 2 + 1) * P]
                            for k, kt in enumerate(keys(q)):
                                last = mm(o_, Vt[:, kt, g * HD:(g + 1) * HD], PT[:, k, h, :],
                                          start=(k == 0), stop=(k == nk - 1))
                        pr.close(last, f"o{q}{g}")

                    lora1(0)
                    prepare(0)
                    prepare_next = {}
                    attention_inputs()
                    invert(0)
                    solve(0)
                    prepare(1)
                    invert(1)
                    solve(1)
                    lora1(1)
                    prepare(2)
                    invert(2)
                    solve(2)
                    prepare(3)
                    invert(3)
                    solve(3)
                    for q, g in ATT_GROUPS:
                        att_scores(q, g)
                        att_values(q, g)

                    pr.copied(pe, "y3_1")
                    for c in range(2):
                        b = pr.open(pe, f"mean{c}")
                        pr.close(mm(b[:, 0:T], heads, ys[:, c, :], start=True, stop=True), f"mean{c}")
                    for c in range(2):
                        head_sum(f"var{c}", Z[:, c, :], "ysq_ready", c + 1)

                    pe.wait_ge(sem("mix_ready"), 2)
                    for g in range(2):
                        for q in range(3):
                            pr.copied(pe, f"o{q}{g}")
                    for u in range(N_OUT):
                        w = piece(n)
                        for j in range(UC // P):
                            name = f"out{u * UC // P + j}"
                            b = pr.open(pe, name)
                            for c in range(KC):
                                last = mm(b[:, 0:T], w[:, c, j * P:(j + 1) * P], mixT[:, c, :],
                                          start=(c == 0), stop=(c == KC - 1))
                            pr.close(last, name)
                        piece_free[n] = (f"bank_filled{pr.place[name][0]}", pr.place[name][1])
                        n += 1

                    pe.wait_ge(sem("sq_ready"), 2)
                    channel_sum("ss2", ones, sq, range(KC))
                    pe.wait_ge(sem("h_ready"), 2)
                    b = pr.open(pe, "route")
                    for t in range(TILES):
                        for c in range(KC):
                            last = mm(b[:, t * 36:(t + 1) * 36], h2T[:, c, t * P:(t + 1) * P], rtw[:, c, :],
                                      start=(c == 0), stop=(c == KC - 1))
                    pr.close(last, "route")
                    for t in range(TILES):
                        for j in range(2):
                            b = pr.open(pe, f"htok{t}{j}")
                            for i in range(4):
                                last = nc.tensor.transpose(b[:, i * P:(i + 1) * P],
                                                           h2T[:, 4 * j + i, t * P:(t + 1) * P], ident)
                            pr.close(last, f"htok{t}{j}")
                    pe.wait_ge(sem("asg_ready"), 1)
                    b = pr.open(pe, "pos")
                    asg3 = [asg[:, t, :, :] for t in range(TILES)]
                    for t in range(TILES):
                        for e in range(t + 1):
                            last = mm(b[:, t * N_EXP:(t + 1) * N_EXP], ck("before", P) if e == t else ones, asg3[e],
                                      start=(e == 0), stop=(e == t))
                    for e in range(TILES):
                        last = mm(b[:, T:T + N_EXP], ones, asg3[e], start=(e == 0), stop=(e == TILES - 1))
                    pr.close(last, "pos")

                @block.sync
                def _(sp):
                    def load(n, src):
                        if n >= 2:
                            s, v = piece_free[n - 2]
                            sp.wait_ge(sem(s), v)
                        sp.dma_start(stream[n % 2], src.rearrange("(c p) n -> p c n", p=P))\
                          .then_inc(sem(f"piece_loaded{n % 2}"), 16)

                    rows = bass.ds(layer * D, D)
                    for n in range(N_MOD):
                        load(n, a["w_mod"][rows, n * UC:(n + 1) * UC])
                    for m, u in enumerate(IN_ORDER):
                        load(N_MOD + m, a["w_in"][rows, u * UC:(u + 1) * UC])
                    for u in range(N_OUT):
                        load(N_MOD + N_IN + u, a["w_out"][rows, u * UC:(u + 1) * UC])
                    pr.copied(sp, "in10")
                    sp.dma_start(o["kT"][bass.ds(layer * P, P), :], kT[:, 0:TP]).then_inc(sem("stored"), 16)
                    pr.copied(sp, "in11")
                    sp.dma_start(o["vT"][bass.ds(layer * P, P), :], vT[:, 0:TP]).then_inc(sem("stored"), 16)
                    for l in range(4):
                        pr.copied(sp, f"state{l}_0")
                    sp.dma_start(o["state"][bass.ds(layer * P, P), :], Sout.rearrange("p l v -> p (l v)"))\
                      .then_inc(sem("stored"), 16)
                    sp.wait_ge(sem("stored"), 48)

                @block.gpsimd
                def _(pool):
                    L = Lane(pool, "pool_steps")
                    g = nc.gpsimd
                    for c in (0, COL[1] - 1, W - 1):
                        L.step(g.memset(hT[:, :, c:c + 1], 0.0), hold=False)
                        for v in (slab, conv):
                            L.step(g.memset(v[:, :, c:c + 1], 0.0), hold=False)
                    L.step(g.memset(S0c, 0.0), hold=False)
                    for t in range(1, TILES):
                        L.step(g.memset(Sg[:, t * 129:t * 129 + 1], 0.0), hold=t == TILES - 1)
                    L.sig(g.memset(Sg[:, 0:1], 0.0), "pads_ready")
                    for l, (d, c) in enumerate(LANES):
                        for t in range(TILES):
                            for h in range(2):
                                pr.copied(pool, f"g{l}_{t}_{h}")
                        for lev in range(LEVELS):
                            if lev >= 2:
                                pr.filled(pool, f"t1_{l}_{lev - 2}_1")
                                if lev == 2:
                                    pool.wait_ge(sem("x_ready"), 2 * l + 2)
                            elif l:
                                pr.filled(pool, f"t1_{l - 1}_{LEVELS - 2 + lev}_1")
                            m = ck("level", P, (d * LEVELS + lev) * P)[:, None, :].to_broadcast([P, 2, P])
                            for t in range(TILES):
                                ins = g.tensor_tensor(Nl[lev % 2][:, 2 * t:2 * t + 2, :], G[:, t, :, 0, 0, :], m, ALU.mult)
                                if t < TILES - 1:
                                    L.step(ins, hold=False)
                                else:
                                    L.sig(ins, "level_ready")

                @block.scalar
                def _(act):
                    L = Lane(act, "act_steps")
                    f = nc.scalar.activation
                    s = sem("small_loaded")
                    rows = bass.ds(layer * P, P)
                    for dst, name in ((par[:, :], "par"), (w1a1.rearrange("p d k m -> p (d k m)"), "w1a1"),
                                      (w2a2.rearrange("p d m -> p (d m)"), "w2a2"),
                                      (rtw.rearrange("p c e -> p (c e)"), "rtw"),
                                      (S0.rearrange("p l v -> p (l v)"), "s0"), (kT[:, 3 * P:4 * P], "ck"),
                                      (Vt[:, 3, :], "cv")):
                        act.dma_start(dst, a[name][rows, :]).then_inc(s, 16)

                    L.sig(f(sq[:, :, :], xT[:, :, :], ACT.Square), "sq_ready")

                    def norm(n):
                        b = pr.filled(act, f"ss{n}")
                        L.free(f(ss[:, :], b[:, 0:T], ACT.Sqrt, bias=ck("eps", 1), scale=1.0 / D), pr, f"ss{n}", hold=False)
                        act.wait_ge(sem("n_ready"), n)
                        for c in range(KC):
                            for st in range(2):
                                cols, pad = STREAMS[st]
                                dst = hT[:, c, pad] if n == 1 else h2T[:, c, cols]
                                ins = f(dst, n1[:, c, cols], ACT.Identity, bias=mod[:, (0, 24)[n - 1] + c, st:st + 1],
                                        scale=gain[:, n - 1, c, st:st + 1])
                                if c == KC - 1 and st == 1:
                                    L.sig(ins, "h_ready")
                                else:
                                    L.step(ins, hold=False)

                    act.wait_ge(sem("pads_ready"), 1)
                    norm(1)
                    for u in IN_ORDER:
                        for j in range(2):
                            i = 2 * u + j
                            b = pr.filled(act, f"in{i}")
                            full = b[:, 0:W - 2]
                            if 12 <= i < 20:
                                L.free(f(slab[:, i - 12, 1:W - 1], full, ACT.Copy), pr, f"in{i}", hold=False)
                                continue
                            if i < 6:
                                L.free(f(conv[:, i, 1:W - 1], full, ACT.Copy), pr, f"in{i}", hold=False)
                                continue
                            dst, fn = ((gate[:, i - 20, :], ACT.Sigmoid) if i >= 20 else
                                       (qT[:, i - 6, :], ACT.Copy) if i < 10 else (vT, ACT.Copy))
                            prompt, sample = b[:, 0:TP], b[:, 1 + TP:1 + T]
                            if i == 10:
                                L.step(f(kT[:, 0:TP], prompt, ACT.Copy), hold=False)
                                ins = f(kraw, sample, ACT.Copy)
                            else:
                                L.step(f(dst[:, 0:TP], prompt, fn), hold=False)
                                ins = f(dst[:, TP:T], sample, fn)
                            L.free(ins, pr, f"in{i}", hold=False)

                    def lora1(d):
                        b = pr.filled(act, f"lora1_{d}")
                        L.step(f(lora[d][HALF[0], :], b[HALF[0], 0:T], ACT.Tanh), hold=False)
                        L.free(f(lora[d][HALF[1], :], b[HALF[1], 0:T], ACT.Copy), pr, f"lora1_{d}", hold=False)

                    def prepare(l):
                        d, c = LANES[l]
                        i = 2 * d + c
                        if l:
                            act.wait_ge(sem("decayed_ready"), l)
                        b = pr.filled(act, f"decay{l}")
                        L.free(f(Sg.rearrange("p (t q) -> p t q", t=TILES)[:, :, 1:129],
                                 b[:, 0:T].rearrange("p (t q) -> p t q", t=TILES), ACT.Sigmoid,
                                 bias=pk("w0", i)), pr, f"decay{l}", hold=False)
                        b = pr.filled(act, f"rate{l}")
                        L.free(f(A_, b[:, 0:T], ACT.Sigmoid, bias=pk("a0", i)), pr, f"rate{l}", hold=False)
                        act.wait_ge(sem("kv_ready"), l + 1)
                        if l:
                            pr.filled(act, f"norm{l - 1}")
                        L.sig(f(t1, K_, ACT.Square, scale=pk("kk", i)), "ksq_ready", hold=False)
                        b = pr.filled(act, f"norm{l}")
                        L.free(f(rn, b[:, 0:T], ACT.Sqrt), pr, f"norm{l}", hold=False)
                        b = pr.filled(act, f"tokv{l}")
                        L.free(f(tok[l % 2][:, 0, :, :], b[:, 0:T].rearrange("p (t q) -> p t q", t=TILES), ACT.Copy),
                               pr, f"tokv{l}", hold=False)
                        act.wait_ge(sem("sums_ready"), l + 1)
                        L.step(f(Ep, Lp, ACT.Exp, scale=-DECAY), hold=False)
                        L.sig(f(Em, Lp, ACT.Exp, scale=DECAY), "exp_ready", hold=False)
                        for w, name in ((1, "tokb"), (2, "tokk")):
                            b = pr.filled(act, f"{name}{l}")
                            L.free(f(tok[l % 2][:, w, :, :], b[:, 0:T].rearrange("p (t q) -> p t q", t=TILES), ACT.Copy),
                                   pr, f"{name}{l}", hold=False)

                    def invert(l):
                        for lev in range(1, LEVELS):
                            for half in range(2):
                                name = f"t1_{l}_{lev}_{half}"
                                b = pr.filled(act, name)
                                L.free(f(T1[:, 3 * half:3 * half + 3, :], b[:, 0:T].rearrange("p (i q) -> p i q", i=3),
                                         ACT.Copy), pr, name, hold=False)

                    def solve(l):
                        d, c = LANES[l]
                        for n_, t in enumerate(TILE_ORDER[d]):
                            b = pr.filled(act, f"rhs{l}_{t}")
                            L.free(f(rhs, b[:, 0:P], ACT.Copy), pr, f"rhs{l}_{t}", hold=False)
                            b = pr.filled(act, f"sa{l}_{t}")
                            L.free(f(SA, b[:, 0:P], ACT.Copy), pr, f"sa{l}_{t}", hold=False)

                    def attention_inputs():
                        b = pr.filled(act, "vtok")
                        L.free(f(Vt[:, 0:3, :], b[:, 0:T].rearrange("p (t q) -> p t q", t=3), ACT.Copy), pr, "vtok",
                               hold=False)
                        for g in range(2):
                            b = pr.filled(act, f"kdup{g}")
                            L.free(f(Kd[:, g, :], b[:, :], ACT.Copy), pr, f"kdup{g}", hold=False)

                    def attention(q, g):
                        nk = len(keys(q)) * P
                        n_ = ATT_GROUPS.index((q, g))
                        act.wait_ge(sem("negm_ready"), n_ + 1)
                        for h in range(4):
                            name = f"s{q}{g}{h % 2}" if q == 0 else f"s{q}{g}{h}"
                            off = (h // 2) * P if q == 0 else 0
                            src = bank[pr.place[name][0]][:, off:off + nk]
                            ins = f(Pm[:, h, 0:nk], src, ACT.Exp, bias=negm[:, h:h + 1], scale=HD ** -0.5,
                                    accum_out=sums[:, h:h + 1])
                            if q == 0 and h < 2:
                                L.step(ins, hold=False)
                            else:
                                L.free(ins, pr, name, hold=False)
                        L.sig(f(esink, esink, ACT.Exp), "exps_ready", hold=False)
                        for k in range(len(keys(q))):
                            name = f"pt{q}{g}{k}"
                            b = pr.filled(act, name)
                            L.free(f(PT[:, k, :, :], b[:, :].rearrange("p (h q) -> p h q", h=4), ACT.Copy), pr, name,
                                   hold=False)

                    lora1(0)
                    prepare(0)
                    attention_inputs()
                    invert(0)
                    solve(0)
                    prepare(1)
                    invert(1)
                    solve(1)
                    lora1(1)
                    prepare(2)
                    invert(2)
                    solve(2)
                    prepare(3)
                    invert(3)
                    solve(3)

                    for q, g in ATT_GROUPS:
                        attention(q, g)
                    for c in range(2):
                        b = pr.filled(act, f"var{c}")
                        L.free(f((rn, A_)[c], b[:, 0:T], ACT.Sqrt, bias=ck("eps", 1, 1), scale=1.0 / HD), pr, f"var{c}",
                               hold=False)
                    pr.copied(act, "out7")
                    L.sig(f(sq[:, :, :], xT[:, :, :], ACT.Square), "sq_ready")
                    norm(2)
                    act.wait_ge(sem("gx_ready"), 1)
                    L.sig(f(gx, gx, ACT.Exp), "gexp_ready", hold=False)
                    for t in range(TILES):
                        for j in range(2):
                            b = pr.filled(act, f"htok{t}{j}")
                            L.free(f(h2tok[:, t, j * 512:(j + 1) * 512], b[:, :], ACT.Copy), pr, f"htok{t}{j}", hold=False)
                    act.wait_ge(sem("e21_ready"), 1)
                    L.sig(f(e21, e21, ACT.Exp), "e21exp_ready", hold=False)

                @block.vector
                def _(dve):
                    L = Lane(dve, "dve_steps")
                    v = nc.vector
                    tt, ts, stt = v.tensor_tensor, v.tensor_scalar, v.scalar_tensor_tensor

                    def wide(x, n):
                        return x[:, :, None].to_broadcast([P, x.shape[1], n])

                    dve.wait_ge(sem("small_loaded"), 16 * 7)
                    L.step(ts(negmu, pk("mu", 8, 8), -1.0, None, ALU.mult), hold=False)
                    L.step(ts(omka, pk("ka", 0, 4), -1.0, 1.0, ALU.mult, ALU.add), hold=False)
                    b = pr.filled(dve, "mod")
                    L.free(tt(mod, b[:, 0:96].rearrange("p (j s) -> p j s", s=2), wide(pk("b_mod", 0, 48), 2), ALU.add),
                           pr, "mod")
                    for n, (first, name) in enumerate(((8, "norm_mix"), (32, "norm_ffn"))):
                        L.step(stt(gain[:, n, :, :], mod[:, first:first + 8, :], 1.0, wide(pk(name, 0, 8), 2),
                                   ALU.add, ALU.mult))

                    def norm(n):
                        pr.copied(dve, f"ss{n}")
                        L.step(v.reciprocal(rstd, ss))
                        L.sig(tt(n1[:, :, :], xT[:, :, :], rstd[:, None, :].to_broadcast([P, KC, T]), ALU.mult),
                              "n_ready")

                    norm(1)
                    for i in range(12, 20):
                        pr.copied(dve, f"in{i}")
                    L.step(tt(diff, slab[:, :, 0:W - 1], slab[:, :, 1:W], ALU.subtract))

                    def shifted(dst, d, j, name=None):
                        for n, (cols, pad) in enumerate(STREAMS):
                            behind = slice(pad.start - 1 + d, pad.stop - 1 + d)
                            mu = negmu[:, j:j + 1] if d else pk("mu", j)
                            ins = stt(dst[:, cols], diff[:, j, behind], mu, slab[:, j, pad], ALU.mult, ALU.add)
                            if n and name:
                                L.sig(ins, name, hold=False)
                            else:
                                L.step(ins, hold=False)

                    def z_inputs(d):
                        if d:
                            pr.filled(dve, "lora1_0")
                        shifted(Z[:, 0, :], d, 6)
                        shifted(Z[:, 1, :], d, 7, "z_ready")

                    def tiles3(x):
                        return x.rearrange("p (t q) -> p t q", t=TILES)

                    def prepare(l):
                        d, c = LANES[l]
                        i, q = 2 * d + c, l % 2
                        shifted(K_, d, 2 + c, "kv_ready")
                        if l:
                            pr.filled(dve, f"tokv{l - 1}")
                        shifted(V_, d, 4 + c, "v_ready")
                        shifted(R_, d, c)
                        pr.copied(dve, f"decay{l}")
                        if l:
                            dve.wait_ge(sem("exp_ready"), l)
                        L.step(v.tensor_tensor_scan(Lp, ck("reset", 3 * 129), Sg, 0.0, ALU.mult, ALU.add))
                        L.step(v.tensor_copy(cmid, tiles3(Lp)[:, :, 64]))
                        L.sig(tt(tiles3(Lp), tiles3(Lp), wide(cmid, 129), ALU.subtract), "sums_ready", hold=False)
                        pr.copied(dve, f"norm{l}")
                        L.step(ts(rn, rn, 1e-12, None, ALU.max))
                        L.step(v.reciprocal(rn, rn))
                        L.step(stt(kkn, K_, pk("kk", i), rn, ALU.mult, ALU.mult))
                        pr.copied(dve, f"rate{l}")
                        L.step(tt(rn, kkn, A_, ALU.mult), hold=False)
                        if l:
                            pr.filled(dve, f"bon{l - 1}")
                        L.step(ts(t2, A_, pk("ka", i), omka[:, i:i + 1], ALU.mult, ALU.add))
                        L.step(tt(K_, K_, t2, ALU.mult))
                        L.sig(stt(t2, R_, pk("rk", i), K_, ALU.mult, ALU.mult), "rk_ready", hold=False)
                        dve.wait_ge(sem("exp_ready"), l + 1)
                        E3, M3 = tiles3(Ep), tiles3(Em)
                        if d == 0:
                            ea, er, eb = E3[:, :, 0:P], E3[:, :, 1:1 + P], M3[:, :, 1:1 + P]
                            e_mid, e_end = M3[:, :, 0], E3[:, :, P]
                        else:
                            ea, er, eb = M3[:, :, 1:1 + P], M3[:, :, 0:P], E3[:, :, 0:P]
                            e_mid, e_end = E3[:, :, P], M3[:, :, 0]
                        L.step(v.tensor_copy(ec[:, l, 0, :], e_mid), hold=False)
                        L.step(v.tensor_copy(ec[:, l, 1, :], e_end), hold=False)
                        L.step(stt(AR[q][:, :, 0, :], tiles3(kkn), -1.0, ea, ALU.mult, ALU.mult), hold=False)
                        L.step(tt(AR[q][:, :, 1, :], tiles3(R_), er, ALU.mult), hold=False)
                        L.step(tt(tiles3(BT[q]), tiles3(rn), eb, ALU.mult), hold=False)
                        L.sig(tt(tiles3(KT[q]), tiles3(K_), eb, ALU.mult), "decayed_ready")
                        b = pr.filled(dve, f"bon{l}")
                        if d == 0:
                            L.free(tt(bonus[:, c, :], b[:, 0:T], V_, ALU.mult), pr, f"bon{l}", hold=False)
                        else:
                            L.free(tt(t2, b[:, 0:T], V_, ALU.mult), pr, f"bon{l}")
                            L.step(tt(bonus[:, c, :], bonus[:, c, :], t2, ALU.add), hold=False)
                        m = ck("tri", 2 * P, 2 * P * d)[:, None, :].to_broadcast([P, 2, 2 * P])
                        for t in range(TILES):
                            for h in range(2):
                                b = pr.filled(dve, f"g{l}_{t}_{h}")
                                L.free(tt(G[:, t, h, :, :, :].rearrange("p w a q -> p w (a q)"),
                                          b[:, :].rearrange("p (w q) -> p w q", w=2), m, ALU.mult),
                                       pr, f"g{l}_{t}_{h}", hold=False)

                    def invert(l):
                        eye = ident[:, None, :].to_broadcast([P, 3, P])
                        dve.wait_ge(sem("level_ready"), l * LEVELS + 1)
                        for lev in range(LEVELS):
                            for half in range(2):
                                ii = slice(3 * half, 3 * half + 3)
                                if lev == 0:
                                    name = f"t1_{l}_0_{half}"
                                    b = pr.filled(dve, name)
                                    L.free(tt(X_[:, ii, :], b[:, 0:T].rearrange("p (i q) -> p i q", i=3), eye, ALU.add),
                                           pr, name, hold=False)
                                    L.sig(tt(XT[:, ii, :], Nl[0][:, ii, :], eye, ALU.add), "x_ready")
                                    continue
                                for what, x in (("dx", X_), ("dxt", XT)):
                                    if what == "dx" and lev == LEVELS - 1:
                                        continue
                                    name = f"{what}_{l}_{lev}_{half}"
                                    b = pr.filled(dve, name)
                                    L.free(tt(x[:, ii, :], x[:, ii, :], b[:, 0:T].rearrange("p (i q) -> p i q", i=3),
                                              ALU.add), pr, name, hold=False)

                    def solve(l):
                        d, c = LANES[l]
                        order = TILE_ORDER[d]
                        for h in range(2):
                            ins = ts(S0c[HALF[h], HALF[h]], S0[HALF[h], l, :], ec[HALF[h], l, 0, order[1]:order[1] + 1], None,
                                     ALU.mult)
                            if h:
                                L.sig(ins, "seed_ready")
                            else:
                                L.step(ins, hold=False)
                        for n_, t in enumerate(order):
                            if n_ < 2:
                                b = pr.filled(dve, f"state{l}_{t}")
                                end = ec[:, l, 1, t:t + 1]
                                if n_ == 0:
                                    L.free(ts(Sout[:, l, :], b[:, 0:HD], end, None, ALU.mult), pr, f"state{l}_{t}",
                                           hold=False)
                                else:
                                    L.step(tt(stmp[HALF[0], :], b[HALF[0], 0:HD], S0c[HALF[0], HALF[0]], ALU.add), hold=False)
                                    L.free(tt(stmp[HALF[1], :], b[HALF[1], 0:HD], S0c[HALF[1], HALF[1]], ALU.add), pr,
                                           f"state{l}_{t}")
                            b = pr.filled(dve, f"y{l}_{t}")
                            dst = ys[:, c, t * P:(t + 1) * P]
                            if d == 0:
                                L.free(v.tensor_copy(dst, b[:, 0:P]), pr, f"y{l}_{t}", hold=False)
                            else:
                                L.free(tt(dst, dst, b[:, 0:P], ALU.add), pr, f"y{l}_{t}", hold=False)
                            if n_ == 1:
                                nt = order[2]
                                for h in range(2):
                                    ins = ts(S0c[HALF[h], HALF[h]], stmp[HALF[h], :], ec[HALF[h], l, 1, t:t + 1],
                                             ec[HALF[h], l, 0, nt:nt + 1], ALU.mult, ALU.mult)
                                    if h:
                                        L.sig(ins, "seed_ready")
                                    else:
                                        L.step(ins, hold=False)

                    def short_conv():
                        for i in range(6):
                            pr.copied(dve, f"in{i}")
                        L.step(tt(conv[:, 2:4, :], conv[:, 2:4, :], conv[:, 4:6, :], ALU.mult))
                        for c in range(2):
                            u, acc = conv[:, 2 + c, :], conv[:, 4 + c, 1:W - 1]
                            L.step(ts(acc, u[:, 0:W - 2], pk("conv_w", c), None, ALU.mult))
                            L.step(stt(acc, u[:, 1:W - 1], pk("conv_w", 2 + c), acc, ALU.mult, ALU.add))
                            L.step(stt(acc, u[:, 2:W], pk("conv_w", 4 + c), acc, ALU.mult, ALU.add))
                            for cols, pad in STREAMS:
                                L.step(tt(mixT[:, c, cols], conv[:, 4 + c, pad], conv[:, c, pad], ALU.mult), hold=False)

                    def attention_inputs():
                        cos, sin = ck("cos", TS), ck("sin", TS)
                        b = pr.filled(dve, "swapk")
                        L.free(tt(rtmp[:, 0:TS], b[:, 0:TS], sin, ALU.mult), pr, "swapk", hold=False)
                        L.step(tt(kT[:, TP:T], kraw, cos, ALU.mult))
                        L.sig(tt(kT[:, TP:T], kT[:, TP:T], rtmp[:, 0:TS], ALU.add), "k_roped")
                        for j in range(2):
                            b = pr.filled(dve, f"swapq{j}")
                            r2 = rtmp[:, 512 * j:512 * j + 512].rearrange("p (c t) -> p c t", c=2) if False else \
                                rtmp.rearrange("p (j c t) -> p j c t", j=2, c=2)[:, j]
                            q2 = qT[:, 2 * j:2 * j + 2, TP:T]
                            L.free(tt(r2, b[:, :].rearrange("p (c t) -> p c t", c=2),
                                      sin[:, None, :].to_broadcast([P, 2, TS]), ALU.mult), pr, f"swapq{j}", hold=False)
                            L.step(tt(q2, q2, cos[:, None, :].to_broadcast([P, 2, TS]), ALU.mult))
                            L.sig(tt(q2, q2, r2, ALU.add), "q_roped", hold=False)

                    def attention(q, g):
                        sink = pk("sink", 4 * g, 4)
                        if q == 0:
                            for par_ in range(2):
                                b = pr.filled(dve, f"s{q}{g}{par_}")
                                L.step(v.reduce_max(mx.rearrange("p (c h) -> p h c", h=2)[:, par_, :],
                                                    b[:, 0:2 * P].rearrange("p (c k) -> p c k", c=2), AX.X), hold=par_ == 1)
                        else:
                            for h in range(4):
                                b = pr.filled(dve, f"s{q}{g}{h}")
                                L.step(v.reduce_max(mx[:, h:h + 1], b[:, 0:3 * P], AX.X), hold=h == 3)
                        L.step(stt(mx, mx, HD ** -0.5, sink, ALU.mult, ALU.max))
                        L.step(ts(negm, mx, -1.0, None, ALU.mult))
                        L.sig(tt(esink, sink, negm, ALU.add), "negm_ready")
                        dve.wait_ge(sem("exps_ready"), ATT_GROUPS.index((q, g)) + 1)
                        L.step(tt(rden, sums, esink, ALU.add))
                        L.step(v.reciprocal(rden, rden))
                        nk = len(keys(q)) * P
                        for h in range(4):
                            ins = ts(Pm[:, h, 0:nk], Pm[:, h, 0:nk], rden[:, h:h + 1], None, ALU.mult)
                            if h < 3:
                                L.step(ins, hold=False)
                            else:
                                L.sig(ins, "p_ready", hold=False)
                        b = pr.filled(dve, f"o{q}{g}")
                        L.free(v.tensor_copy(mixT[:, 2 + 2 * g:4 + 2 * g, q * P:(q + 1) * P],
                                             b[:, 0:2 * P].rearrange("p (c q) -> p c q", c=2)), pr, f"o{q}{g}", hold=False)

                    z_inputs(0)
                    prepare(0)
                    attention_inputs()
                    short_conv()
                    invert(0)
                    solve(0)
                    prepare(1)
                    invert(1)
                    solve(1)
                    z_inputs(1)
                    prepare(2)
                    invert(2)
                    solve(2)
                    prepare(3)
                    invert(3)
                    solve(3)
                    for q, g in ATT_GROUPS:
                        attention(q, g)

                    for c in range(2):
                        b = pr.filled(dve, f"mean{c}")
                        L.free(stt(ys[:, c, :], b[:, 0:T], -1.0 / HD, ys[:, c, :], ALU.mult, ALU.add), pr, f"mean{c}")
                        L.sig(tt(Z[:, c, :], ys[:, c, :], ys[:, c, :], ALU.mult), "ysq_ready", hold=False)
                    for c in range(2):
                        y, r = ys[:, c, :], (rn, A_)[c]
                        pr.copied(dve, f"var{c}")
                        L.step(v.reciprocal(r, r))
                        L.step(tt(y, y, r, ALU.mult))
                        L.step(ts(y, y, pk("ln_g", c), pk("ln_b", c), ALU.mult, ALU.add))
                        L.step(tt(y, y, bonus[:, c, :], ALU.add))
                        L.sig(tt(mixT[:, 6 + c, :], y, gate[:, c, :], ALU.mult), "mix_ready", hold=False)

                    for j in range(KC):
                        b = pr.filled(dve, f"out{j}")
                        for st, (cols, _) in enumerate(STREAMS):
                            ins = stt(xT[:, j, cols], b[:, cols], mod[:, 16 + j, st:st + 1], xT[:, j, cols],
                                      ALU.mult, ALU.add)
                            if st:
                                L.free(ins, pr, f"out{j}", hold=False)
                            else:
                                L.step(ins, hold=False)
                    pr.copied(dve, "out7")
                    norm(2)

                    def first_best(out, x, m, n, rev):
                        L.step(v.reduce_max(m, x, AX.X))
                        L.step(tt(out, x, wide(m, n), ALU.is_equal))
                        L.step(tt(out, out, rev[:, None, :].to_broadcast([P, TILES, n]), ALU.mult))
                        L.step(v.reduce_max(gs, out, AX.X))
                        L.step(tt(out, out, wide(gs, n), ALU.is_equal))

                    b = pr.filled(dve, "route")
                    L.free(tt(lg, b[:, 0:TILES * 36].rearrange("p (t e) -> p t e", t=TILES),
                              pk("rt_b", 0, 36)[:, None, :].to_broadcast([P, TILES, 36]), ALU.add), pr, "route")
                    first_best(goh, lg[:, :, 0:4], gm, 4, ck("rev", 4, 4))
                    L.sig(tt(gx, lg[:, :, 0:4], wide(gm, 4), ALU.subtract), "gx_ready")
                    lge = lg[:, :, 4:36].rearrange("p t (g e) -> p t g e", g=N_GROUPS)
                    for t in range(TILES):
                        L.step(tt(el4[:, t, :, :], lge[:, t, :, :], wide(goh[:, t, :], EPG), ALU.mult), hold=t == TILES - 1)
                    L.step(v.reduce_sum(el, el4.rearrange("p t g e -> p t e g"), AX.X))
                    first_best(oh1, el, m1, EPG, ck("rev", EPG))
                    L.step(stt(el, oh1, -3e38, el, ALU.mult, ALU.add))
                    first_best(oh2, el, m2, EPG, ck("rev", EPG))
                    L.sig(tt(e21, m2, m1, ALU.subtract), "e21_ready")
                    dve.wait_ge(sem("gexp_ready"), 1)
                    L.step(v.reduce_sum(gs, gx, AX.X))
                    dve.wait_ge(sem("e21exp_ready"), 1)
                    L.step(ts(w1_, e21, 1.0, None, ALU.add))
                    L.step(tt(w1_, w1_, gs, ALU.mult))
                    L.step(v.reciprocal(w1_, w1_))
                    L.step(tt(w2_, w1_, e21, ALU.mult))
                    L.step(tt(tw, oh1, wide(w1_, EPG), ALU.mult), hold=False)
                    L.step(tt(el, oh2, wide(w2_, EPG), ALU.mult))
                    L.step(tt(tw, tw, el, ALU.add), hold=False)
                    L.step(tt(oh1, oh1, oh2, ALU.add))
                    for t in range(TILES):
                        e8 = oh1[:, t, None, :].to_broadcast([P, N_GROUPS, EPG])
                        w8 = tw[:, t, None, :].to_broadcast([P, N_GROUPS, EPG])
                        g8 = wide(goh[:, t, :], EPG)
                        L.step(tt(wall3[:, t, :].rearrange("p (g e) -> p g e", g=N_GROUPS), g8, w8, ALU.mult), hold=False)
                        ins = tt(asg[:, t, :, :], g8, e8, ALU.mult)
                        if t < TILES - 1:
                            L.step(ins, hold=False)
                        else:
                            L.sig(ins, "asg_ready")
                    b = pr.filled(dve, "pos")
                    flat = asg.rearrange("p t g e -> p (t g e)")
                    L.step(stt(posm[:, :], b[:, 0:TILES * N_EXP], 1.0, flat, ALU.add, ALU.mult))
                    L.step(ts(posm[:, :], posm[:, :], -1.0, None, ALU.add), hold=False)
                    L.free(v.reduce_max(rnd[:, 7:8], b[:, T:T + N_EXP], AX.X), pr, "pos")
                    for k in range(1, MAX_ROUNDS):
                        L.step(ts(rnd[:, k:k + 1], rnd[:, 7:8], float(k * SLOTS), None, ALU.is_gt), hold=k == MAX_ROUNDS - 1)
                    L.step(v.reduce_sum(rnd[:, 0:1], rnd[:, 1:MAX_ROUNDS], AX.X))
                    L.step(ts(rounds_i[:, :], rnd[:, 0:1], 1.0, None, ALU.add))

        def segments(c):
            at_, out = c * T, []
            while at_ < (c + 1) * T:
                n = min((c + 1) * T, (at_ // 512 + 1) * 512) - at_
                out.append((at_ // 512, at_ % 512, at_ - c * T, n))
                at_ += n
            return out

        def open_sums():
            with nc.Block() as block:
                @block.vector
                def _(dve):
                    nc.vector.memset(WselT, 0.0).then_inc(sem("zero_ready"), 1)

                @block.tensor
                def _(pe):
                    pe.wait_ge(sem("zero_ready"), 1)
                    for i in range(6):
                        nc.tensor.matmul(bank[i][:, :], WselT[:, 0:P], const[:, 0:512], start=True, stop=True)

        PAIRS = N_EXP // 2

        def experts_round(layer):
            IN_PAIR = 4
            A_UP, A_WT, A_TOK, A_DOWN = 1, 2, 3, 4
            B_UP, B_HT, B_DOWN, B_TOK = 1, 2, 3, 4
            LAST = PAIRS - 1
            bA, bB = bank[6], bank[7]
            js = "p j s -> p (j s)"

            with nc.Block() as block:
                def full_a(eng, i, k):
                    eng.wait_ge(sem("a_filled"), i * IN_PAIR + (k + 1))

                def full_b(eng, i, k):
                    eng.wait_ge(sem("b_filled"), i * IN_PAIR + (k + 1))

                def emptied_a(eng, i, k):
                    eng.wait_ge(sem("a_emptied"), i * IN_PAIR + (k + 1))

                def emptied_b(eng, i, k):
                    eng.wait_ge(sem("b_emptied"), i * IN_PAIR + (k + 1))

                def pairs(eng, body):
                    with eng.Fori(0, LAST) as i:
                        body(i, False)
                    body(LAST, True)

                @block.sync
                def _(sp):
                    def load(i, m, j):
                        name, rows = (("exp_w1", D), ("exp_w3", D), ("exp_w2", DE))[m]
                        src = a[name][bass.ds((layer * N_EXP + i * 2 + j) * rows, rows), :]
                        sp.dma_start(unit[2 * m + j].rearrange("p (c n) -> p c n", c=rows // P),
                                     src.rearrange("(c p) n -> p c n", p=P)).then_inc(sem(f"unit{2 * m + j}"), 16)

                    for m in range(3):
                        for j in range(2):
                            load(0, m, j)
                    with sp.Fori(1, PAIRS) as i:
                        for m in range(3):
                            if m == 0:
                                full_a(sp, i - 1, A_UP)
                            else:
                                full_b(sp, i - 1, B_UP if m == 1 else B_DOWN)
                            for j in range(2):
                                load(i, m, j)

                @block.tensor
                def _(pe):
                    mm = nc.tensor.matmul

                    def gather(half):
                        b = bB if half else bA
                        for c in range(4):
                            for t in range(TILES):
                                last = mm(b[:, c * P:(c + 1) * P], h2tok[:, t, (4 * half + c) * P:(4 * half + c + 1) * P],
                                          Sel[:, t, :, :].rearrange(js), start=(t == 0), stop=(t == TILES - 1))
                        last.then_inc(sem("b_filled" if half else "a_filled"), 1)

                    def loaded(i, m, j):
                        pe.wait_ge(sem(f"unit{2 * m + j}"), i * 16 + 16)

                    def up(i):
                        emptied_a(pe, i, 0)
                        for m, b in ((0, bA), (1, bB)):
                            for j in range(2):
                                loaded(i, m, j)
                            if m:
                                emptied_b(pe, i, 0)
                            for c in range(KC):
                                if c == 4 and not m:
                                    emptied_b(pe, i, 0)
                                for j in range(2):
                                    last = mm(b[HALF[j], :], Xg[:, c, j, :], unit[2 * m + j][:, c * DE:(c + 1) * DE],
                                              start=(c == 0), stop=(c == KC - 1))
                            last.then_inc(sem("b_filled" if m else "a_filled"), 1)

                    def scatter():
                        for c in range(KC):
                            for bk, col, t0, n in segments(c):
                                mm(bank[bk][:, col:col + n], yg[:, c * P:(c + 1) * P], WselT[:, t0:t0 + n],
                                   start=False, stop=True, skip_group_check=True)

                    def down(i, half, last_pair):
                        b = bB if half else bA
                        for f_ in range(FC):
                            for j in range(2):
                                lo = f_ * D + half * 512
                                last = mm(b[HALF[j], :], hidT[:, f_, j, :], unit[4 + j][:, lo:lo + 512],
                                          start=(f_ == 0), stop=(f_ == FC - 1))
                        last.then_inc(sem("b_filled" if half else "a_filled"), 1)

                    def rest(i, last_pair):
                        pe.wait_ge(sem("wsel_ready"), i + 1)
                        emptied_a(pe, i, A_UP)
                        for t in range(TILES):
                            last = nc.tensor.transpose(bA[:, t * P:(t + 1) * P], Wsel[:, t, :, :].rearrange(js), ident)
                        last.then_inc(sem("a_filled"), 1)
                        emptied_b(pe, i, B_UP)
                        for f_ in range(FC):
                            last = nc.tensor.transpose(bB[:, f_ * P:(f_ + 1) * P], hid[:, f_ * P:(f_ + 1) * P], ident)
                        last.then_inc(sem("b_filled"), 1)
                        emptied_a(pe, i, A_WT)
                        if not last_pair:
                            pe.wait_ge(sem("sel_ready"), i + 2)
                            gather(0)
                        for j in range(2):
                            loaded(i, 2, j)
                        emptied_b(pe, i, B_HT)
                        if not last_pair:
                            emptied_a(pe, i, A_TOK)
                        down(i, 0, last_pair)
                        down(i, 1, last_pair)
                        if not last_pair:
                            emptied_b(pe, i, B_DOWN)
                            gather(1)

                    pe.wait_ge(sem("sel_ready"), 1)
                    gather(0)
                    gather(1)
                    up(0)
                    rest(0, False)
                    with pe.Fori(1, LAST) as i:
                        up(i)
                        scatter()
                        rest(i, False)
                    up(LAST)
                    scatter()
                    rest(LAST, True)
                    emptied_a(pe, LAST, A_DOWN - 1)
                    emptied_b(pe, LAST, B_DOWN)
                    scatter()

                @block.vector
                def _(dve):
                    v = nc.vector

                    def select(i):
                        pair = bass.ds(i * 2, 2)
                        iota = ck("iota", SLOTS)[:, None, :].to_broadcast([P, 2, SLOTS])
                        for t in range(TILES):
                            ins = v.tensor_tensor(Sel[:, t, :, :], iota,
                                                  pos3[:, t, pair][:, :, None].to_broadcast([P, 2, SLOTS]), ALU.is_equal)
                        ins.then_inc(sem("sel_ready"), 1)
                        dve.wait_ge(sem("sel_ready"), i + 1)

                    def tokens(i, k):
                        full_b(dve, i, k)
                        v.tensor_copy(Xg[:, 4:8, :, :].rearrange("p c j s -> p c (j s)"),
                                      bB[:, :].rearrange("p (c s) -> p c s", c=4)).then_inc(sem("b_emptied"), 1)

                    def body(i, last_pair):
                        pair = bass.ds(i * 2, 2)
                        for t in range(TILES):
                            ins = v.tensor_tensor(Wsel[:, t, :, :], Sel[:, t, :, :],
                                                  wall3[:, t, pair][:, :, None].to_broadcast([P, 2, SLOTS]), ALU.mult)
                        ins.then_inc(sem("wsel_ready"), 1)
                        if not last_pair:
                            dve.wait_ge(sem("wsel_ready"), i + 1)
                            select(i + 1)
                        full_b(dve, i, B_UP)
                        emptied_a(dve, i, A_UP)
                        v.tensor_tensor(hid, sil, bB[:, :], ALU.mult).then_inc(sem("b_emptied"), 1)
                        full_b(dve, i, B_HT)
                        v.tensor_copy(hidT.rearrange("p f j s -> p (f j s)"), bB[:, :]).then_inc(sem("b_emptied"), 1)
                        full_b(dve, i, B_DOWN)
                        v.tensor_copy(yg[:, 512:], bB[:, :]).then_inc(sem("b_emptied"), 1)
                        if not last_pair:
                            tokens(i, B_TOK)

                    select(0)
                    tokens(0, 0)
                    pairs(dve, body)
                    v.tensor_scalar(posm[:, :], posm[:, :], float(-SLOTS), None, ALU.add).then_inc(sem("pos_moved"), 1)

                @block.scalar
                def _(act):
                    f = nc.scalar.activation

                    def tokens(i, k):
                        full_a(act, i, k)
                        f(Xg[:, 0:4, :, :].rearrange("p c j s -> p c (j s)"),
                          bA[:, :].rearrange("p (c s) -> p c s", c=4), ACT.Copy).then_inc(sem("a_emptied"), 1)

                    def body(i, last_pair):
                        full_a(act, i, A_UP)
                        f(sil, bA[:, :], ACT.Silu).then_inc(sem("a_emptied"), 1)
                        full_a(act, i, A_WT)
                        f(WselT, bA[:, 0:T], ACT.Copy).then_inc(sem("a_emptied"), 1)
                        if not last_pair:
                            tokens(i, A_TOK)
                        full_a(act, i, A_DOWN - 1 if last_pair else A_DOWN)
                        f(yg[:, 0:512], bA[:, :], ACT.Copy).then_inc(sem("a_emptied"), 1)

                    tokens(0, 0)
                    pairs(act, body)

        def close_sums():
            with nc.Block() as block:
                @block.vector
                def _(dve):
                    for c in range(KC):
                        for bk, col, t0, n in segments(c):
                            for st, (cols, _) in enumerate(STREAMS):
                                lo, hi = max(t0, cols.start), min(t0 + n, cols.stop)
                                if lo < hi:
                                    nc.vector.scalar_tensor_tensor(
                                        xT[:, c, lo:hi], bank[bk][:, col + lo - t0:col + hi - t0],
                                        mod[:, 40 + c, st:st + 1], xT[:, c, lo:hi], ALU.mult, ALU.add)

        def final_stage():
            with nc.Block() as block:
                @block.scalar
                def _(act):
                    f = nc.scalar.activation
                    f(sq[:, :, :], xT[:, :, :], ACT.Square).then_inc(sem("sq_ready"), 1)
                    act.wait_ge(sem("ss_filled"), 1)
                    f(ss[:, :], bank[0][:, 0:T], ACT.Sqrt, bias=ck("eps", 1), scale=1.0 / D).then_inc(sem("std_ready"), 1)

                @block.tensor
                def _(pe):
                    pe.wait_ge(sem("sq_ready"), 1)
                    for c in range(KC):
                        last = nc.tensor.matmul(bank[0][:, 0:T], ones, sq[:, c, :], start=(c == 0), stop=(c == KC - 1))
                    last.then_inc(sem("ss_filled"), 1)

                @block.vector
                def _(dve):
                    dve.wait_ge(sem("std_ready"), 1)
                    nc.vector.reciprocal(rstd, ss).then_inc(sem("rstd_ready"), 1)
                    dve.wait_ge(sem("rstd_ready"), 1)
                    for c in range(KC):
                        nc.vector.scalar_tensor_tensor(h2T[:, c, :], xT[:, c, :], nout[:, c:c + 1], rstd,
                                                       ALU.mult, ALU.mult).then_inc(sem("y_ready"), 1)

                @block.sync
                def _(sp):
                    sp.wait_ge(sem("y_ready"), KC)
                    sp.dma_start(o["yT"], h2T.rearrange("p c t -> p (c t)")).then_inc(sem("stored"), 16)
                    sp.wait_ge(sem("stored"), 16)

        with nc.Block() as block:
            s_const, s_cond = sem("const_loaded"), sem("cond_loaded")

            @block.sync
            def _(sp):
                sp.dma_start(x_sb[:, :], a["xT"]).then_inc(s_const, 16)
                sp.dma_start(const[:, :], a["const"]).then_inc(s_const, 16)
                sp.dma_start(nout[:, :], a["nout"]).then_inc(s_const, 16)
                sp.wait_ge(s_const, 48)

            @block.scalar
            def _(act):
                act.dma_start(cond[:, :], a["cond"]).then_inc(s_cond, 16)
                act.wait_ge(s_cond, 16)
                nc.scalar.activation(scond[:, :], cond[:, :], ACT.Silu)

        clear(list(sems.values()))

        with nc.Fori(0, DEPTH) as layer:
            mixer_stage(layer)
            clear(list(sems.values()))
            open_sums()
            n_rounds = nc.values_load(rounds_i[0:1, 0:1], min_val=1, max_val=MAX_ROUNDS)
            clear(list(sems.values()))
            with nc.Fori(0, n_rounds):
                experts_round(layer)
                clear(list(sems.values()))
            close_sums()
            clear(list(sems.values()))
        final_stage()


def constants():
    i = np.arange(P)
    s, t = i[:, None], i[None, :]
    out = np.zeros((P, NCK), np.float32)

    def put(name, x, off=0):
        out[:, CK[name] + off:CK[name] + off + x.shape[1]] = x

    put("ident", s == t)
    put("ones", np.ones((P, P)))
    put("heads", s // HD == t // HD)
    put("before", s < t)
    put("swap", np.where((t % 32 < 16) & (s == t + 16), -1.0, np.where((t % 32 >= 16) & (s == t - 16), 1.0, 0.0)))
    for g in range(2):
        put("dup", s == g * HD + t % HD, g * P)
    inv = np.float32(10000.0) ** (-np.arange(0, 32, 2, dtype=np.float32) / np.float32(32))
    tok = np.arange(TS)
    pos = np.where((i % HD < 32)[:, None], (tok // 64)[None, :], (tok % 64)[None, :]).astype(np.float32)
    ang = pos * inv[i % 16][:, None].astype(np.float32)
    put("cos", np.cos(ang))
    put("sin", np.sin(ang))
    put("att", np.where(t > s, -1e30, 0.0))
    put("att", np.where(t < s, -1e30, 0.0), P)
    for n, m in enumerate((s < t, s <= t, s > t, s >= t)):
        put("tri", m, n * P)
    for lev in range(LEVELS):
        put("level", ((t >> lev) & 1 == 1) & (s >> lev == (t >> lev) - 1), lev * P)
        put("level", ((t >> lev) & 1 == 0) & (s >> lev == (t >> lev) + 1), (LEVELS + lev) * P)
    put("reset", np.tile((np.arange(3 * 129) % 129 != 0)[None, :], (P, 1)))
    put("iota", np.tile(np.arange(SLOTS)[None, :], (P, 1)))
    put("rev", np.tile(np.arange(EPG, 0, -1)[None, :], (P, 1)))
    put("eps", np.tile(np.array([[NORM_EPS, GN_EPS]]), (P, 1)))
    return out


def layouts(i):
    L = DEPTH
    cat = np.concatenate

    def chunks(x, n):
        return np.swapaxes(x.reshape(*x.shape[:-1], n, P), -1, -2)

    def rows(x):
        return np.ascontiguousarray(x.reshape(L * P, -1))

    x = cat([i["x_prompt"][0], i["x_sample"][0]], 0)
    cond = np.stack([i["c_ctx"], i["c"][0]], 0)
    per = []
    for l in range(L):
        def two(n):
            return chunks(i[n][l], 2).transpose(1, 0, 2).reshape(P, 4)
        per.append(cat([
            chunks(i["b_mod"][l], 48), chunks(i["norm_mix"][l], 8), chunks(i["norm_ffn"][l], 8),
            chunks(i["conv_w"][l], 2).transpose(1, 0, 2).reshape(P, 6),
            chunks(i["rw_mu"][l], 8).transpose(1, 0, 2).reshape(P, 16),
            two("rw_w0"), two("rw_a0"), two("rw_kk"), two("rw_ka"), two("rw_rk"),
            chunks(i["rw_ln_g"][l], 2), chunks(i["rw_ln_b"][l], 2),
            np.broadcast_to(i["attn_sink"][l], (P, 8)),
            np.broadcast_to(cat([i["rt_group_b"][l], i["rt_exp_b"][l]]), (P, 36))], 1))
    w1a1 = cat([i["rw_w1"], i["rw_a1"]], -1).reshape(L, 2, 2, P, P).transpose(0, 3, 1, 2, 4)
    w2a2 = cat([i["rw_w2"], i["rw_a2"]], 2).transpose(0, 2, 1, 3)
    rtw = cat([i["rt_group_w"], i["rt_exp_w"]], -1).reshape(L, KC, P, 36).transpose(0, 2, 1, 3)
    s0 = i["state_wkv"][0].reshape(L, 2, 2, 2, HD, HD).transpose(0, 3, 5, 1, 2, 4)
    return {
        "xT": chunks(x, KC).transpose(1, 2, 0).reshape(P, KC * T),
        "cond": chunks(cond, KC).transpose(1, 2, 0).reshape(P, 2 * KC),
        "const": constants(),
        "nout": chunks(i["norm_out"], KC),
        "par": rows(np.stack(per)), "w1a1": rows(w1a1), "w2a2": rows(w2a2), "rtw": rows(rtw), "s0": rows(s0),
        "ck": rows(i["cache_k"][0].reshape(L, P, KV).transpose(0, 2, 1)),
        "cv": rows(i["cache_v"][0].reshape(L, P, KV)),
        "w_mod": i["w_mod"].reshape(L * D, 6 * D), "w_in": i["w_in"].reshape(L * D, IN_W),
        "w_out": i["w_out"].reshape(L * D, D),
        "exp_w1": i["exp_w1"].reshape(L * N_EXP * D, DE), "exp_w3": i["exp_w3"].reshape(L * N_EXP * D, DE),
        "exp_w2": i["exp_w2"].reshape(L * N_EXP * DE, D),
    }


OUTS = {"yT": (P, KC * T), "kT": (DEPTH * P, TP), "vT": (DEPTH * P, TP), "state": (DEPTH * P, 4 * HD)}


def kernel(**inputs):
    import concourse.bacc as bacc
    from concourse.bass_utils import run_bass_kernel_spmd as run

    nc = bacc.Bacc("TRN2", target_bir_lowering=False, num_devices=1)
    arrays = {f"in_{k}": np.ascontiguousarray(v) for k, v in layouts({k: np.asarray(v) for k, v in inputs.items()}).items()}
    a = {k[3:]: nc.dram_tensor(k, v.shape, F32, kind="ExternalInput").ap() for k, v in arrays.items()}
    o = {k: nc.dram_tensor(f"out_{k}", s, F32, kind="ExternalOutput").ap() for k, s in OUTS.items()}
    build(nc, a, o)
    r = run(nc, [arrays], core_ids=[0]).results[0]
    y = r["out_yT"].reshape(P, KC, T).transpose(2, 1, 0).reshape(T, D)
    k, v = (r[f"out_{n}"].reshape(DEPTH, P, TP).transpose(0, 2, 1).reshape(1, DEPTH, TP, 2, HD) for n in ("kT", "vT"))
    state = r["out_state"].reshape(DEPTH, 2, HD, 2, 2, HD).transpose(0, 3, 4, 1, 5, 2)
    return y[None, :TP].copy(), y[None, TP:].copy(), k.copy(), v.copy(), state.reshape(1, DEPTH, 2, 4, HD, HD).copy()
```

```python
import numpy as np
import concourse.bass as bass
from concourse import mybir
from contextlib import ExitStack

F32 = mybir.dt.float32
I32 = mybir.dt.int32
ACT = mybir.ActivationFunctionType
ALU = mybir.AluOpType
AX = mybir.AxisListType

P = 128
DEPTH = 2
D = 1024
KC = D // P
TP, TS = 128, 256
T = TP + TS
TILES = T // P
W = T + 3
COL = (1, 2 + TP)
HD = 64
CONV, ATT, KV, RW = 256, 512, 128, 256
IN_W = 3 * CONV + ATT + 2 * KV + 5 * RW
N_GROUPS, EPG = 4, 8
N_EXP = N_GROUPS * EPG
DE = D // 2
FC = DE // P
SLOTS = 64
MAX_ROUNDS = T // SLOTS
DECAY = 0.6065306597126334
NORM_EPS, GN_EPS = 1e-6, 64e-5
LEVELS = 7
UC = 256

PK, _n = {}, 0
for _name, _w in (("b_mod", 48), ("norm_mix", 8), ("norm_ffn", 8), ("conv_w", 6), ("mu", 16), ("w0", 4),
                  ("a0", 4), ("kk", 4), ("ka", 4), ("rk", 4), ("ln_g", 2), ("ln_b", 2), ("sink", 8), ("rt_b", 36)):
    PK[_name] = _n
    _n += _w
NPK = _n

CK, _n = {}, 0
for _name, _w in (("ident", P), ("ones", P), ("heads", P), ("before", P), ("swap", P), ("pick", 2 * P - 2),
                  ("cos", TS), ("sin", TS), ("att", 2 * P), ("tri", 4 * P), ("level", 2 * LEVELS * P),
                  ("reset", 3 * 129), ("iota", SLOTS), ("rev", EPG), ("eps", 2)):
    CK[_name] = _n
    _n += _w
NCK = _n


def build(nc, a, o):
    ctx = ExitStack()
    with ctx:
        def sb(name, cols, dt=F32):
            return ctx.enter_context(nc.sbuf_tensor(name, [P, cols], dt))

        sems = {}

        def sem(name):
            if name not in sems:
                sems[name] = ctx.enter_context(nc.semaphore(name))
            return sems[name]

        x_sb = sb("x_sb", KC * T)
        xT = x_sb[:, :].rearrange("p (c t) -> p c t", c=KC)
        const = sb("const", NCK)
        par = sb("par", NPK)
        nout = sb("nout", KC)
        cond = sb("cond", 2 * KC)
        mod_sb = sb("mod_sb", 96)
        mod = mod_sb[:, :].rearrange("p (j s) -> p j s", s=2)
        gains = sb("gains", 32)
        gain = gains[:, :].rearrange("p (n c s) -> p n c s", n=2, s=2)
        posm = sb("posm", TILES * N_EXP)
        wall = sb("wall", TILES * N_EXP)
        rounds_i = sb("rounds_i", 1, I32)
        AR_N = 45080
        arena = sb("arena", AR_N)

        bank = [ctx.enter_context(nc.psum_tensor(f"bank{i}", [P, 512], F32)) for i in range(8)]

        def ck(name, n, off=0):
            return const[:, CK[name] + off:CK[name] + off + n]

        def pk(name, i=0, n=1):
            return par[:, PK[name] + i:PK[name] + i + n]

        ident, ones, heads = ck("ident", P), ck("ones", P), ck("heads", P)

        at = [0]

        def take(n):
            at[0] += n
            assert at[0] <= AR_N, at[0]
            return arena[:, at[0] - n:at[0]]

        stream = [take(KC * UC).rearrange("p (c n) -> p c n", c=KC) for _ in range(2)]
        h_at = at[0]
        hT = take(KC * W + 4)[:, 0:KC * W].rearrange("p (c w) -> p c w", c=KC)
        Pm, PT = arena[:, h_at:h_at + 768], arena[:, h_at + 768:h_at + 1536]
        slab = take(8 * W).rearrange("p (c w) -> p c w", c=8)
        gate = take(2 * T).rearrange("p (c t) -> p c t", c=2)
        conv_at = at[0]
        conv = take(6 * W).rearrange("p (c w) -> p c w", c=6)
        qT = take(4 * T).rearrange("p (c t) -> p c t", c=4)
        kT = take(512)
        vT = take(T)
        Kd = [[x[:, 0:512], x[:, 512:1024]] for x in (take(1024), arena[:, h_at + 1536:h_at + 2560])]
        Vt = take(4 * P).rearrange("p (t d) -> p t d", t=4)
        mix_at = at[0]
        mixT = take(KC * T).rearrange("p (c t) -> p c t", c=KC)
        kraw = mixT[:, 2, 0:TS]
        rtmp = mixT[:, 5:8, :].rearrange("p c t -> p (c t)")[:, 0:1024]
        diff = take(8 * (W - 1)).rearrange("p (c w) -> p c w", c=8)
        Z = take(2 * T).rearrange("p (c t) -> p c t", c=2)
        R_, K_, V_ = take(T), take(T), take(T)
        lora = [take(T), take(T)]
        Sg = take(3 * 129)
        Lp = take(3 * 129)
        Ep, Em = take(3 * 129), take(3 * 129)
        A_, kkn, rn, t1, t2 = take(T), take(T), take(T), take(T), take(T)
        AR = [take(3 * 256).rearrange("p (t a q) -> p t a q", t=3, a=2) for _ in range(2)]
        BK = [[take(T) for _ in range(2)] for _ in range(2)]
        tok = [take(3 * T).rearrange("p (w t d) -> p w t d", w=3, t=3) for _ in range(2)]
        ec = take(4 * 6).rearrange("p (l w t) -> p l w t", l=4, w=2)
        bonus = take(2 * T).rearrange("p (c t) -> p c t", c=2)
        ys = take(2 * T).rearrange("p (c t) -> p c t", c=2)
        G = take(6 * 512).rearrange("p (t h w a q) -> p t h w a q", t=3, h=2, w=2, a=2)
        X_, XT = (take(6 * P).rearrange("p (i q) -> p i q", i=6) for _ in range(2))
        T1 = arena[:, conv_at:conv_at + 6 * P].rearrange("p (i q) -> p i q", i=6)
        Nl = [take(6 * P).rearrange("p (i q) -> p i q", i=6) for _ in range(2)]
        zeros = X_.rearrange("p i q -> p (i q)")[:, 0:512]
        mod_at = at[0] - 12 * P - 12 * P - 6 * 512
        mod_stream = [arena[:, mod_at + i * 2048:mod_at + (i + 1) * 2048].rearrange("p (c n) -> p c n", c=KC)
                      for i in range(2)]
        mod_part = [arena[:, mod_at + 4096 + i * UC:mod_at + 4096 + (i + 1) * UC] for i in range(2)]
        scond = arena[:, mod_at + 4608:mod_at + 4608 + KC * 32].rearrange("p (c s) -> p c s", c=KC)
        S0 = take(4 * HD).rearrange("p (l v) -> p l v", l=4)
        S0c = take(P)
        Sout = take(4 * HD).rearrange("p (l v) -> p l v", l=4)
        rhs = take(P)
        SA = take(P)
        ss, rstd = R_, K_
        stmp = take(HD)
        cmid = take(TILES)
        w1a1 = take(2 * 2 * P).rearrange("p (d k m) -> p d k m", d=2, k=2)
        w2a2 = take(2 * RW).rearrange("p (d m) -> p d m", d=2)
        rtw = take(KC * 36).rearrange("p (c e) -> p c e", c=KC)
        negmu, omka = take(8), take(4)
        mx, sums, negm, esink, rden = take(4), take(4), take(4), take(4), take(4)
        sq = mixT
        n1 = mixT
        h2T = arena[:, h_at:h_at + KC * T].rearrange("p (c t) -> p c t", c=KC)
        r_at = [h_at + KC * T + 24]

        def rt(n):
            r_at[0] += n
            return arena[:, r_at[0] - n:r_at[0]]

        lg = rt(TILES * 36).rearrange("p (t e) -> p t e", t=TILES)
        gm, gs = rt(TILES), rt(TILES)
        gx = rt(TILES * 4).rearrange("p (t g) -> p t g", t=TILES)
        goh = rt(TILES * 4).rearrange("p (t g) -> p t g", t=TILES)
        el4 = rt(TILES * N_EXP).rearrange("p (t g e) -> p t g e", t=TILES, g=N_GROUPS)
        el = rt(TILES * EPG).rearrange("p (t e) -> p t e", t=TILES)
        oh1 = rt(TILES * EPG).rearrange("p (t e) -> p t e", t=TILES)
        oh2 = rt(TILES * EPG).rearrange("p (t e) -> p t e", t=TILES)
        tw = rt(TILES * EPG).rearrange("p (t e) -> p t e", t=TILES)
        m1, m2, e21, w1_, w2_ = rt(TILES), rt(TILES), rt(TILES), rt(TILES), rt(TILES)
        asg = rt(TILES * N_EXP).rearrange("p (t g e) -> p t g e", t=TILES, g=N_GROUPS)
        rnd = rt(8)
        assert r_at[0] <= mix_at

        unit = [arena[:, i * 4096:(i + 1) * 4096] for i in range(2)]
        h2tok = arena[:, mix_at:mix_at + TILES * D].rearrange("p (t d) -> p t d", t=TILES)
        assert 2 * 4096 <= mix_at
        m_at = mix_at + TILES * D
        unit = [arena[:, m_at + i * 4096:m_at + (i + 1) * 4096] for i in (2, 3)] + unit + \
               [arena[:, m_at + i * 4096:m_at + (i + 1) * 4096] for i in (0, 1)]
        m_at += 4 * 4096
        e_at = [2 * 4096]

        def moe(n):
            if e_at[0] + n > mix_at and e_at[0] < m_at:
                e_at[0] = m_at
            e_at[0] += n
            assert e_at[0] <= AR_N
            return arena[:, e_at[0] - n:e_at[0]]

        Sel = moe(TILES * P).rearrange("p (t j s) -> p t j s", t=TILES, j=2)
        Wsel = moe(TILES * P).rearrange("p (t j s) -> p t j s", t=TILES, j=2)
        WselT = moe(T)
        Xg = moe(KC * P).rearrange("p (c j s) -> p c j s", c=KC, j=2)
        sil, hid = moe(DE), moe(DE)
        hidT = moe(FC * P).rearrange("p (f j s) -> p f j s", f=FC, j=2)
        yg = moe(D)

        pos3 = posm[:, :].rearrange("p (t e) -> p t e", t=TILES)
        wall3 = wall[:, :].rearrange("p (t e) -> p t e", t=TILES)

        def clear(block_sems):
            with nc.Block() as block:
                @block.sync
                def _(sp):
                    for s in block_sems:
                        sp.sem_clear(s)

        class Lane:

            def __init__(self, eng, name):
                self.eng, self.s, self.n, self.counts = eng, sem(name), 0, {}

            def step(self, ins, hold=True):
                self.n += 1
                ins.then_inc(self.s, 1)
                if hold:
                    self.eng.wait_ge(self.s, self.n)

            def sig(self, ins, name, hold=True):
                self.counts[name] = self.counts.get(name, 0) + 1
                ins.then_inc(sem(name), 1)
                if hold:
                    self.eng.wait_ge(sem(name), self.counts[name])

            def free(self, ins, turns, name, hold=True):
                ins.then_inc(sem(f"bank_emptied{turns.place[name][0]}"), 1)
                if hold:
                    turns.copied(self.eng, name)

        class PsumTurns:

            def __init__(self, banks):
                self.banks, self.n, self.count, self.place = banks, 0, {}, {}

            def open(self, pe, name, b=None):
                if b is None:
                    b = self.banks[self.n % len(self.banks)]
                    self.n += 1
                if self.count.get(b):
                    pe.wait_ge(sem(f"bank_emptied{b}"), self.count[b])
                self.count[b] = self.count.get(b, 0) + 1
                self.place[name] = (b, self.count[b])
                return bank[b]

            def close(self, last, name):
                last.then_inc(sem(f"bank_filled{self.place[name][0]}"), 1)

            def filled(self, eng, name):
                b, n = self.place[name]
                eng.wait_ge(sem(f"bank_filled{b}"), n)
                return bank[b]

            def copied(self, eng, name):
                b, n = self.place[name]
                eng.wait_ge(sem(f"bank_emptied{b}"), n)

        HALF = (slice(0, HD), slice(HD, P))
        STREAMS = ((slice(0, TP), slice(1, 1 + TP)), (slice(TP, T), slice(2 + TP, 2 + T)))
        LANES = [(d, c) for d in range(2) for c in range(2)]
        TILE_ORDER = ((0, 1, 2), (0, 2, 1))
        UNITS = [(0, g, (0, 1, 2, 3)) for g in range(2)] + \
                [(q, g, hs) for q in (1, 2) for g in range(2) for hs in ((0, 1), (2, 3))]
        N_MOD, N_IN, N_OUT = 6 * D // UC, IN_W // UC, D // UC
        SUM_BANKS = KC * T // 512
        N_MOD1 = 2 * D // UC
        IN_ORDER = (6, 7, 8, 9, 10, 0, 1, 2, 3, 4, 5)
        MOD_WITH = [[m for m in range(N_MOD1, N_MOD) if (m - N_MOD1) * 8 // (N_MOD - N_MOD1) == k] for k in range(N_IN)]

        FRONT = 9
        SOLVE = ("rhs", "sa", "out")

        def in_turn(do):
            def lane(l, fill):
                fill = list(fill)

                def next_fill():
                    for step in (fill.pop(0) if fill else ()):
                        do(*step)

                do("scores", l)
                next_fill()
                for lev in range(LEVELS):
                    do("level", l, lev)
                    next_fill()
                for n in range(TILES):
                    for step in SOLVE:
                        do("solve", l, n, step)
                        next_fill()
                assert not fill

            def front(l, k):
                return [("front", l, k)] if k < FRONT else []

            units = [[("att_scores", 0)]]
            for u in range(len(UNITS)):
                units += [[("att_scale", u)], [("att_turn", u)], [("att_values", u)]]
                if u + 1 < len(UNITS):
                    units[-1].append(("att_scores", u + 1))
            units.reverse()

            def att():
                return units.pop() if units else []

            def out(j):
                return [("out_part", 0, j)]

            for k, steps in enumerate(((0,), (1,), (2,), (3, 4), (5, 6), (7,))):
                do("project", IN_ORDER[5 + k // 2], k % 2)
                for step in steps:
                    do("front", 0, step)
                if k % 2:
                    do("mod_with", 5 + k // 2)
            do("front", 0, 8)
            do("mod_done")
            inputs = [[("project", u, j)] for u in IN_ORDER[8:] for j in range(2)]
            lane(0, [[("short_conv",)], inputs[0]] + [inputs[k + 1] + front(1, k) for k in range(5)] +
                 [front(1, 5), front(1, 6), front(1, 7), front(1, 8) + [("att_inputs", 0)], [("att_inputs", 1)],
                  [("att_inputs", 2)], [("shift_inputs", 1)], att(), att(), att()])
            lane(1, [att() + front(2, k) for k in range(17)])
            lane(2, [att() + front(3, k) for k in range(11)] + [out(0), [], out(1)])
            lane(3, [out(2)] + [[]] * LEVELS + [out(3), [], out(4), [], out(5)])
            assert not units

        def keys(q):
            return (0,) if q == 0 else (1, 2, 3)

        def segments(c):
            at_, out = c * T, []
            while at_ < (c + 1) * T:
                n = min((c + 1) * T, (at_ // 512 + 1) * 512) - at_
                out.append((at_ // 512, at_ % 512, at_ - c * T, n))
                at_ += n
            return out

        def add_experts(done=None):
            for c in range(KC):
                for bk, col, t0, n in segments(c):
                    for st, (cols, _) in enumerate(STREAMS):
                        lo, hi = max(t0, cols.start), min(t0 + n, cols.stop)
                        if lo < hi:
                            ins = nc.vector.scalar_tensor_tensor(
                                xT[:, c, lo:hi], bank[bk][:, col + lo - t0:col + hi - t0],
                                mod[:, 40 + c, st:st + 1], xT[:, c, lo:hi], ALU.mult, ALU.add)
                if done:
                    done(ins)

        def mixer_stage(layer):
            pr = PsumTurns(list(range(5)))
            att_turn = [0]

            def att_bank():
                att_turn[0] += 1
                return 5 + (att_turn[0] - 1) % 3

            piece_free = {}

            with nc.Block() as block:
                @block.tensor
                def _(pe):
                    mm = nc.tensor.matmul

                    def piece(n):
                        pe.wait_ge(sem(f"piece_loaded{n % 2}"), 16 * (n // 2 + 1))
                        return stream[n % 2]

                    def mod_piece(n):
                        pe.wait_ge(sem(f"mod_loaded{n % 2}"), 16 * (n // 2 + 1))
                        b = pr.open(pe, f"mod{n}", 6 if n < N_MOD1 else None)
                        for c in range(KC):
                            g = c % 4
                            last = mm(b[32 * g:32 * g + 32, 0:UC], scond[:, c, :], mod_stream[n % 2][:, c, :],
                                      start=(c < 4), stop=(c >= 4))
                        pr.close(last, f"mod{n}")

                    def mod_turn(n):
                        name = "mod_first" if n < N_MOD1 else "mod_rest"
                        pr.copied(pe, f"mod{n}")
                        if n in (0, N_MOD1):
                            pr.open(pe, name, 7)
                        for j in range(UC // P):
                            first = n in (0, N_MOD1) and j == 0
                            end = n in (N_MOD1 - 1, N_MOD - 1) and j == UC // P - 1
                            last = mm(bank[7][:, 0:P], mod_part[n % 2][:, j * P:(j + 1) * P],
                                      ck("pick", P, P - 2 - 2 * (n * UC // P + j)), start=first, stop=end)
                        if n in (N_MOD1 - 1, N_MOD - 1):
                            pr.close(last, name)

                    def channel_sum(name, before, chunks=range(KC)):
                        b = pr.open(pe, name) if 0 in chunks else bank[pr.place[name][0]]
                        for c in chunks:
                            pe.wait_ge(sem("sq_ready"), before + c + 1)
                            last = mm(b[:, 0:T], ones, sq[:, c, :], start=(c == 0), stop=(c == KC - 1))
                        if KC - 1 in chunks:
                            pr.close(last, name)

                    pe.wait_ge(sem("cond_ready"), 2)
                    for n in range(N_MOD1):
                        mod_piece(n)
                        if n:
                            mod_turn(n - 1)
                        if 1 <= n <= KC // 2:
                            channel_sum("ss1", 0, (2 * n - 2, 2 * n - 1))
                    mod_turn(N_MOD1 - 1)

                    def mod_with(k):
                        for m in MOD_WITH[k]:
                            mod_piece(m)
                            if m > N_MOD1:
                                mod_turn(m - 1)

                    n = 0

                    def project(u, j):
                        nonlocal n
                        w = piece(n) if j == 0 else stream[n % 2]
                        name = f"in{u * UC // P + j}"
                        b = pr.open(pe, name)
                        for c in range(KC):
                            if n == 0 and j == 0:
                                pe.wait_ge(sem("h_ready"), c + 1)
                                pe.wait_ge(sem("h_sample_ready"), c + 1)
                            last = mm(b[:, 0:W - 2], w[:, c, j * P:(j + 1) * P], hT[:, c, 1:W - 1],
                                      start=(c == 0), stop=(c == KC - 1))
                        pr.close(last, name)
                        if j == UC // P - 1:
                            piece_free[n] = (f"bank_filled{pr.place[name][0]}", pr.place[name][1])
                            n += 1

                    for k, u in enumerate(IN_ORDER[0:5]):
                        project(u, 0)
                        project(u, 1)
                        mod_with(k)

                    def lora1(d):
                        pe.wait_ge(sem("z_ready"), d + 1)
                        b = pr.open(pe, f"lora1_{d}")
                        for k in range(2):
                            last = mm(b[:, 0:T], w1a1[:, d, k, :], Z[:, k, :], start=(k == 0), stop=(k == 1))
                        pr.close(last, f"lora1_{d}")

                    def lora2(l):
                        d, c = LANES[l]
                        if c == 0:
                            pr.copied(pe, f"lora1_{d}")
                        for half, name in enumerate(("decay", "rate")):
                            b = pr.open(pe, f"{name}{l}")
                            last = mm(b[:, 0:T], w2a2[:, d, c * P:(c + 1) * P], lora[half], start=True, stop=True)
                            pr.close(last, f"{name}{l}")

                    def head_sum(name, src, ready, count):
                        pe.wait_ge(sem(ready), count)
                        b = pr.open(pe, name)
                        pr.close(mm(b[:, 0:T], heads, src, start=True, stop=True), name)

                    def token_major(l, what, src, ready):
                        pe.wait_ge(sem(ready), l + 1)
                        b = pr.open(pe, f"{what}{l}")
                        for t in range(TILES):
                            last = nc.tensor.transpose(b[:, t * P:(t + 1) * P], src[:, t * P:(t + 1) * P], ident)
                        pr.close(last, f"{what}{l}")

                    def scores(l):
                        q = l % 2
                        pe.wait_ge(sem("padded_ready"), l + 1)
                        for t in range(TILES):
                            for h in range(2):
                                b = pr.open(pe, f"g{l}_{t}_{h}")
                                for w in range(2):
                                    last = mm(b[:, w * 256:(w + 1) * 256], BK[w][h][:, t * P:(t + 1) * P],
                                              AR[q][:, t, :, :], start=True, stop=True)
                                pr.close(last, f"g{l}_{t}_{h}")

                    def front(l, k):
                        if k == 0:
                            if LANES[l][1] == 0:
                                lora1(LANES[l][0])
                            lora2(l)
                        elif k == 1:
                            token_major(l, "tokv", V_, "v_ready")
                        elif k == 3:
                            head_sum(f"norm{l}", t1, "ksq_ready", l + 1)
                        elif k == 8:
                            head_sum(f"bon{l}", t2, "rk_ready", l + 1)
                            token_major(l, "tokb", rn, "decayed_ready")
                            token_major(l, "tokk", K_, "decayed_ready")

                    def level(l, lev):
                        pe.wait_ge(sem("level_ready"), l * LEVELS + lev + 1)
                        for half in range(2):
                            ii = range(3 * half, 3 * half + 3)
                            if lev == 1:
                                pe.wait_ge(sem("x_ready"), 2 * l + half + 1)
                            elif lev:
                                pr.copied(pe, f"dxt_{l}_{lev - 1}_{half}")
                            b = pr.open(pe, f"t1_{l}_{lev}_{half}")
                            for i in ii:
                                last = mm(b[:, (i % 3) * P:(i % 3 + 1) * P], Nl[lev % 2][:, i, :],
                                          X_[:, i, :] if lev else ident, start=True, stop=True)
                            pr.close(last, f"t1_{l}_{lev}_{half}")
                        for half in range(2):
                            ii = range(3 * half, 3 * half + 3)
                            if not lev:
                                continue
                            pr.copied(pe, f"t1_{l}_{lev}_{half}")
                            for what in ("dx", "dxt"):
                                if what == "dx" and lev == LEVELS - 1:
                                    continue
                                b = pr.open(pe, f"{what}_{l}_{lev}_{half}")
                                for i in ii:
                                    o_ = b[:, (i % 3) * P:(i % 3 + 1) * P]
                                    if what == "dx":
                                        last = mm(o_, XT[:, i, :], T1[:, i, :], start=True, stop=True)
                                    else:
                                        last = mm(o_, T1[:, i, :], XT[:, i, :], start=True, stop=True)
                                pr.close(last, f"{what}_{l}_{lev}_{half}")

                    def solve(l, n_, step):
                        d, c = LANES[l]
                        q = l % 2
                        if n_ == 0 and step == "rhs":
                            pr.copied(pe, f"tokk{l}")
                            pr.copied(pe, f"tokb{l}")
                            pr.copied(pe, f"tokv{l}")
                            for half in range(2):
                                pr.copied(pe, f"dxt_{l}_{LEVELS - 1}_{half}")
                        t = TILE_ORDER[d][n_]
                        seeded = n_ > 0
                        vtok, btok, ktok = (tok[q][:, w, t, :] for w in range(3))
                        if step == "rhs":
                            if seeded:
                                pe.wait_ge(sem("seed_ready"), 2 * l + n_)
                            b = pr.open(pe, f"rhs{l}_{t}")
                            for h in range(2):
                                o_ = b[:, h * P:(h + 1) * P]
                                if seeded:
                                    mm(o_, AR[q][:, t, 0, :], S0c, start=True, stop=False)
                                last = mm(o_, G[:, t, h, 1, 0, :], vtok, start=not seeded, stop=True)
                            pr.close(last, f"rhs{l}_{t}")
                            return
                        if step == "sa":
                            pr.copied(pe, f"rhs{l}_{t}")
                            b = pr.open(pe, f"sa{l}_{t}")
                            for h in range(2):
                                last = mm(b[:, h * P:(h + 1) * P], XT[:, 2 * t + h, :], rhs, start=True, stop=True)
                            pr.close(last, f"sa{l}_{t}")
                            return
                        pr.copied(pe, f"sa{l}_{t}")
                        if n_ < 2:
                            b = pr.open(pe, f"state{l}_{t}")
                            for h in range(2):
                                mm(b[HALF[h], 0:HD], btok[:, HALF[h]], SA[:, h * HD:(h + 1) * HD], start=True, stop=True,
                                   skip_group_check=True)
                            for h in range(2):
                                last = mm(b[HALF[h], 0:HD], ktok[:, HALF[h]], vtok[:, HALF[h]], start=False, stop=True,
                                          skip_group_check=True)
                            pr.close(last, f"state{l}_{t}")
                        b = pr.open(pe, f"y{l}_{t}")
                        if seeded:
                            mm(b[:, 0:P], S0c, AR[q][:, t, 1, :], start=True, stop=True, skip_group_check=True)
                        for h in range(2):
                            mm(b[HALF[h], 0:P], vtok[:, HALF[h]], G[:, t, h, 1, 1, :], start=not seeded, stop=True,
                               skip_group_check=True)
                        for h in range(2):
                            last = mm(b[HALF[h], 0:P], SA[:, h * HD:(h + 1) * HD], G[:, t, h, 0, 1, :], start=False,
                                      stop=True, skip_group_check=True)
                        pr.close(last, f"y{l}_{t}")

                    def attention_inputs(k):
                        if k == 0:
                            for i in range(6, 12):
                                pr.copied(pe, f"in{i}")
                            b = pr.open(pe, "swapk")
                            pr.close(mm(b[:, 0:TS], ck("swap", P), kraw[:, :], start=True, stop=True), "swapk")
                            for j in range(2):
                                b = pr.open(pe, f"swapq{j}")
                                for i in range(2):
                                    last = mm(b[:, i * TS:(i + 1) * TS], ck("swap", P), qT[:, 2 * j + i, TP:T],
                                              start=True, stop=True)
                                pr.close(last, f"swapq{j}")
                        elif k == 1:
                            b = pr.open(pe, "vtok")
                            for t in range(TILES):
                                last = nc.tensor.transpose(b[:, t * P:(t + 1) * P], vT[:, t * P:(t + 1) * P], ident)
                            pr.close(last, "vtok")
                        else:
                            pe.wait_ge(sem("k_roped"), 1)
                            for g in range(2):
                                b = pr.open(pe, f"kdup{g}")
                                for h in range(2):
                                    last = mm(b[HALF[h], :], ident[:, HALF[g]], kT[:, :], start=True, stop=True)
                                pr.close(last, f"kdup{g}")

                    def out_part(part, j):
                        nonlocal n
                        name = f"out{part}_{j}"
                        if part == 0:
                            if j == 0:
                                for u in range(len(UNITS)):
                                    pr.copied(pe, f"o{u}")
                            w = piece(n) if j % 2 == 0 else stream[n % 2]
                            col, chunks = j % 2 * P, range(6)
                        else:
                            w = last_out
                            col, chunks = j * P, (6, 7)
                        b = pr.open(pe, name)
                        for c in chunks:
                            last = mm(b[:, 0:T], w[:, c - chunks[0], col:col + P], mixT[:, c, :],
                                      start=(c == chunks[0]), stop=(c == chunks[-1]))
                        pr.close(last, name)
                        if part == 0 and j % 2:
                            piece_free[n] = (f"bank_filled{pr.place[name][0]}", pr.place[name][1])
                            n += 1

                    def att_scores(u):
                        q, g, hs = UNITS[u]
                        if u == 0:
                            pe.wait_ge(sem("q_roped"), 2)
                            pr.copied(pe, "kdup0")
                            pr.copied(pe, "kdup1")
                            pr.copied(pe, "vtok")
                            pe.wait_ge(sem("kd_zero"), 1)
                        for i in range(2):
                            b = pr.open(pe, f"s{u}_{i}", att_bank())
                            if q == 0:
                                for h in (i, i + 2):
                                    last = mm(b[:, (h // 2) * P:(h // 2 + 1) * P], qT[:, 2 * g + h // 2, 0:P],
                                              Kd[g][i][:, 0:P], start=True, stop=True)
                            else:
                                mm(b[:, 0:3 * P], qT[:, 2 * g + hs[0] // 2, q * P:(q + 1) * P], Kd[g][i][:, P:4 * P],
                                   start=True, stop=True)
                                off = (2 - q) * P
                                last = mm(b[:, off:off + P], ident, ck("att", P, (q - 1) * P), start=False, stop=True,
                                          skip_group_check=True)
                            pr.close(last, f"s{u}_{i}")

                    def att_turn(u):
                        q, g, hs = UNITS[u]
                        pe.wait_ge(sem("p_ready"), u + 1)
                        for i, name in enumerate([f"pt{u}_0", f"pt{u}_1"][:1 if q == 0 else 2]):
                            b = pr.open(pe, name, att_bank())
                            n_ = 4 if q == 0 else 3
                            for m in range(n_):
                                last = nc.tensor.transpose(b[:, m * P:(m + 1) * P],
                                                           Pm[:, (i * n_ + m) * P:(i * n_ + m + 1) * P], ident)
                            pr.close(last, name)

                    def att_values(u):
                        q, g, hs = UNITS[u]
                        for name in [f"pt{u}_0", f"pt{u}_1"][:1 if q == 0 else 2]:
                            pr.copied(pe, name)
                        b = pr.open(pe, f"o{u}", att_bank())
                        nk = len(keys(q))
                        for k, kt in enumerate(keys(q)):
                            for i in range(len(hs)):
                                m = i * nk + k
                                last = mm(b[HALF[i % 2], (i // 2) * P:(i // 2 + 1) * P], Vt[:, kt, g * HD:(g + 1) * HD],
                                          PT[:, m * P:(m + 1) * P], start=(k == 0), stop=True, skip_group_check=True)
                        pr.close(last, f"o{u}")

                    steps = {"project": project, "front": front, "scores": scores, "level": level, "solve": solve,
                             "att_inputs": attention_inputs, "att_scores": att_scores, "att_scale": lambda u: None,
                             "att_turn": att_turn, "att_values": att_values, "out_part": out_part,
                             "mod_done": lambda: mod_turn(N_MOD - 1), "short_conv": lambda: None,
                             "mod_with": mod_with, "shift_inputs": lambda d: None}
                    in_turn(lambda what, *which: steps[what](*which))

                    pr.copied(pe, "y3_1")
                    for c in range(2):
                        b = pr.open(pe, f"mean{c}")
                        pr.close(mm(b[:, 0:T], heads, ys[:, c, :], start=True, stop=True), f"mean{c}")
                    for c in range(2):
                        head_sum(f"var{c}", Z[:, c, :], "ysq_ready", c + 1)

                    out_part(0, 6)
                    out_part(0, 7)
                    pe.wait_ge(sem("mix_ready"), 2)
                    def zero_bank(b):
                        pe.wait_ge(sem(f"bank_emptied{b}"), pr.count[b])
                        mm(bank[b][:, :], zeros[:, 0:P], zeros[:, 0:512], start=True, stop=True)

                    last_out = piece(n).rearrange("p c n -> p (c n)").rearrange("p (c n) -> p c n", c=2)
                    for j in range(KC):
                        out_part(1, j)
                    channel_sum("ss2", KC)
                    pe.wait_ge(sem("zero_ready"), 1)
                    for b in range(SUM_BANKS):
                        if b == pr.place["ss2"][0]:
                            continue
                        zero_bank(b)
                    b = pr.open(pe, "route", 7)
                    for t in range(TILES):
                        for c in range(KC):
                            if t == 0:
                                pe.wait_ge(sem("h_ready"), KC + 2 * (c + 1))
                            last = mm(b[:, t * 36:(t + 1) * 36], h2T[:, c, t * P:(t + 1) * P], rtw[:, c, :],
                                      start=(c == 0), stop=(c == KC - 1))
                    pr.close(last, "route")
                    zero_bank(pr.place["ss2"][0])
                    for t in range(TILES):
                        for j in range(2):
                            b = pr.open(pe, f"htok{t}{j}", 6 + j)
                            for i in range(4):
                                last = nc.tensor.transpose(b[:, i * P:(i + 1) * P],
                                                           h2T[:, 4 * j + i, t * P:(t + 1) * P], ident)
                            pr.close(last, f"htok{t}{j}")
                    pe.wait_ge(sem("asg_ready"), 1)
                    b = pr.open(pe, "pos", 6)
                    asg3 = [asg[:, t, :, :] for t in range(TILES)]
                    for t in range(TILES):
                        for e in range(t + 1):
                            last = mm(b[:, t * N_EXP:(t + 1) * N_EXP], ck("before", P) if e == t else ones, asg3[e],
                                      start=(e == 0), stop=(e == t))
                    for e in range(TILES):
                        last = mm(b[:, T:T + N_EXP], ones, asg3[e], start=(e == 0), stop=(e == TILES - 1))
                    pr.close(last, "pos")

                @block.sync
                def _(sp):
                    def load(n, src, dst=None):
                        if n >= 2:
                            s, v = piece_free[n - 2]
                            sp.wait_ge(sem(s), v)
                        sp.dma_start(stream[n % 2] if dst is None else dst, src.rearrange("(c p) n -> p c n", p=P))\
                          .then_inc(sem(f"piece_loaded{n % 2}"), 16)

                    def load_mod(n):
                        if n >= 2:
                            pr.filled(sp, f"mod{n - 2}")
                        sp.dma_start(mod_stream[n % 2],
                                     a["w_mod"][rows, n * UC:(n + 1) * UC].rearrange("(c p) n -> p c n", p=P))\
                          .then_inc(sem(f"mod_loaded{n % 2}"), 16)

                    rows = bass.ds(layer * D, D)
                    for n in range(N_MOD1):
                        load_mod(n)
                    for m, u in enumerate(IN_ORDER):
                        load(m, a["w_in"][rows, u * UC:(u + 1) * UC])
                        for n in MOD_WITH[m]:
                            load_mod(n)
                    for u in range(N_OUT):
                        load(N_IN + u, a["w_out"][bass.ds(layer * D, 6 * P), u * UC:(u + 1) * UC],
                             stream[(N_IN + u) % 2][:, 0:6, :])
                    load(N_IN + N_OUT, a["w_out"][bass.ds(layer * D + 6 * P, 2 * P), :],
                         stream[(N_IN + N_OUT) % 2].rearrange("p c n -> p (c n)").rearrange("p (c n) -> p c n", c=2))
                    sp.wait_ge(sem("mix_ready"), 2)
                    for j in range(2):
                        sp.dma_start(unit[j].rearrange("p (c n) -> p c n", c=KC),
                                     a["exp_w1"][bass.ds((layer * N_EXP + j) * D, D), :]
                                     .rearrange("(c p) n -> p c n", p=P)).then_inc(sem("first_loaded"), 16)
                    pr.filled(sp, f"out1_{KC - 1}")
                    sp.dma_start(unit[2].rearrange("p (c n) -> p c n", c=KC),
                                 a["exp_w3"][bass.ds(layer * N_EXP * D, D), :].rearrange("(c p) n -> p c n", p=P))\
                      .then_inc(sem("first_loaded"), 16)
                    pr.copied(sp, "in10")
                    sp.dma_start(o["kT"][bass.ds(layer * P, P), :], kT[:, 0:TP]).then_inc(sem("stored"), 16)
                    pr.copied(sp, "in11")
                    sp.dma_start(o["vT"][bass.ds(layer * P, P), :], vT[:, 0:TP]).then_inc(sem("stored"), 16)
                    for l in range(4):
                        pr.copied(sp, f"state{l}_0")
                    sp.dma_start(o["state"][bass.ds(layer * P, P), :], Sout.rearrange("p l v -> p (l v)"))\
                      .then_inc(sem("stored"), 16)
                    sp.wait_ge(sem("stored"), 48)
                    sp.wait_ge(sem("first_loaded"), 48)

                @block.gpsimd
                def _(pool):
                    L = Lane(pool, "pool_steps")
                    g = nc.gpsimd
                    L.sig(g.memset(scond[:, :, :], 0.0), "cond_ready", hold=False)
                    for c in (0, COL[1] - 1, W - 1):
                        L.step(g.memset(hT[:, :, c:c + 1], 0.0), hold=False)
                        for v in (slab, conv):
                            L.step(g.memset(v[:, :, c:c + 1], 0.0), hold=False)
                    L.step(g.memset(S0c, 0.0), hold=False)
                    for t in range(1, TILES):
                        L.step(g.memset(Sg[:, t * 129:t * 129 + 1], 0.0), hold=t == TILES - 1)
                    L.sig(g.memset(Sg[:, 0:1], 0.0), "pads_ready")
                    for l, (d, c) in enumerate(LANES):
                        for lev in range(LEVELS):
                            if lev >= 2:
                                pr.filled(pool, f"t1_{l}_{lev - 2}_1")
                                if lev == 2:
                                    pool.wait_ge(sem("x_ready"), 2 * l + 2)
                            elif l:
                                pr.filled(pool, f"t1_{l - 1}_{LEVELS - 2 + lev}_1")
                            m = ck("level", P, (d * LEVELS + lev) * P)[:, None, :].to_broadcast([P, 2, P])
                            for t in range(TILES):
                                if lev == 0:
                                    for h in range(2):
                                        pr.copied(pool, f"g{l}_{t}_{h}")
                                ins = g.tensor_tensor(Nl[lev % 2][:, 2 * t:2 * t + 2, :], G[:, t, :, 0, 0, :], m, ALU.mult)
                                if t < TILES - 1:
                                    L.step(ins, hold=False)
                                else:
                                    L.sig(ins, "level_ready")

                @block.scalar
                def _(act):
                    L = Lane(act, "act_steps")
                    f = nc.scalar.activation
                    s = sem("small_loaded")
                    rows = bass.ds(layer * P, P)
                    for dst, name in ((par[:, :], "par"), (w1a1.rearrange("p d k m -> p (d k m)"), "w1a1"),
                                      (w2a2.rearrange("p d m -> p (d m)"), "w2a2"),
                                      (rtw.rearrange("p c e -> p (c e)"), "rtw"),
                                      (S0.rearrange("p l v -> p (l v)"), "s0"), (kT[:, 3 * P:4 * P], "ck"),
                                      (Vt[:, 3, :], "cv")):
                        act.dma_start(dst, a[name][rows, :]).then_inc(s, 16)

                    act.wait_ge(sem("cond_ready"), 1)
                    f(scond[:, :, 0:2], cond[:, :].rearrange("p (c s) -> p c s", c=KC), ACT.Silu)\
                        .then_inc(sem("cond_ready"), 1)
                    for c in range(KC):
                        act.wait_ge(sem("residual_ready"), c + 1)
                        L.sig(f(sq[:, c, :], xT[:, c, :], ACT.Square), "sq_ready", hold=False)

                    def norm(n):
                        b = pr.filled(act, f"ss{n}")
                        L.free(f(ss[:, :], b[:, 0:T], ACT.Sqrt, bias=ck("eps", 1), scale=1.0 / D), pr, f"ss{n}", hold=False)

                    def modulate(n, streams):
                        act.wait_ge(sem("gain_ready"), n)
                        for c in range(KC):
                            act.wait_ge(sem("n_ready"), 2 if n == 1 else 3 + c)
                            for st in streams:
                                cols, pad = STREAMS[st]
                                dst = hT[:, c, pad] if n == 1 else h2T[:, c, cols]
                                L.sig(f(dst, n1[:, c, cols], ACT.Identity, bias=mod[:, (0, 24)[n - 1] + c, st:st + 1],
                                        scale=gain[:, n - 1, c, st:st + 1]), "h_ready", hold=False)

                    act.wait_ge(sem("pads_ready"), 1)
                    norm(1)
                    modulate(1, (0,))

                    def project(u, j):
                        i = 2 * u + j
                        b = pr.filled(act, f"in{i}")
                        full = b[:, 0:W - 2]
                        if 12 <= i < 20:
                            L.free(f(slab[:, i - 12, 1:W - 1], full, ACT.Copy), pr, f"in{i}", hold=False)
                            return
                        if i < 6:
                            L.free(f(conv[:, i, 1:W - 1], full, ACT.Copy), pr, f"in{i}", hold=False)
                            return
                        dst, fn = ((gate[:, i - 20, :], ACT.Sigmoid) if i >= 20 else
                                   (qT[:, i - 6, :], ACT.Copy) if i < 10 else (vT, ACT.Copy))
                        prompt, sample = b[:, 0:TP], b[:, 1 + TP:1 + T]
                        if i == 10:
                            L.step(f(kT[:, 0:TP], prompt, ACT.Copy), hold=False)
                            ins = f(kraw, sample, ACT.Copy)
                        else:
                            L.step(f(dst[:, 0:TP], prompt, fn), hold=False)
                            ins = f(dst[:, TP:T], sample, fn)
                        L.free(ins, pr, f"in{i}", hold=False)

                    for u in IN_ORDER[0:5]:
                        project(u, 0)
                        project(u, 1)

                    def lora1(d):
                        b = pr.filled(act, f"lora1_{d}")
                        if d:
                            pr.filled(act, "rate1")
                        L.step(f(lora[0][HALF[0], :], b[HALF[0], 0:T], ACT.Tanh), hold=False)
                        L.free(f(lora[1][HALF[1], :], b[HALF[1], 0:T], ACT.Copy), pr, f"lora1_{d}", hold=False)

                    def by_tile(x):
                        return x.rearrange("p (t q) -> p t q", t=TILES)

                    def front(l, k):
                        d, c = LANES[l]
                        i = 2 * d + c
                        if k == 0:
                            if c == 0:
                                lora1(d)
                            if l:
                                act.wait_ge(sem("decayed_ready"), l)
                            b = pr.filled(act, f"decay{l}")
                            L.free(f(by_tile(Sg)[:, :, 1:129], by_tile(b[:, 0:T]), ACT.Sigmoid, bias=pk("w0", i)),
                                   pr, f"decay{l}", hold=False)
                            b = pr.filled(act, f"rate{l}")
                            L.free(f(A_, b[:, 0:T], ACT.Sigmoid, bias=pk("a0", i)), pr, f"rate{l}", hold=False)
                        elif k == 1:
                            act.wait_ge(sem("kv_ready"), l + 1)
                            if l:
                                pr.filled(act, f"norm{l - 1}")
                            L.sig(f(t1, K_, ACT.Square, scale=pk("kk", i)), "ksq_ready", hold=False)
                            b = pr.filled(act, f"tokv{l}")
                            L.free(f(tok[l % 2][:, 0, :, :], by_tile(b[:, 0:T]), ACT.Copy), pr, f"tokv{l}", hold=False)
                        elif k == 2:
                            act.wait_ge(sem("sums_ready"), l + 1)
                            L.step(f(Ep, Lp, ACT.Exp, scale=-DECAY), hold=False)
                            L.sig(f(Em, Lp, ACT.Exp, scale=DECAY), "exp_ready", hold=False)
                        elif k == 3:
                            b = pr.filled(act, f"norm{l}")
                            L.free(f(rn, b[:, 0:T], ACT.Sqrt), pr, f"norm{l}", hold=False)
                        elif k == 8:
                            act.wait_ge(sem("decayed_ready"), l + 1)
                            if l:
                                pr.filled(act, f"g{l - 1}_2_1")
                            for w, src in enumerate((rn, K_)):
                                for h in range(2):
                                    ins = f(BK[w][h][HALF[h], :], src[HALF[h], :], ACT.Copy)
                                    if w and h:
                                        L.sig(ins, "padded_ready", hold=False)
                                    else:
                                        L.step(ins, hold=False)
                            for w, name in ((1, "tokb"), (2, "tokk")):
                                b = pr.filled(act, f"{name}{l}")
                                L.free(f(tok[l % 2][:, w, :, :], by_tile(b[:, 0:T]), ACT.Copy), pr, f"{name}{l}",
                                       hold=False)

                    def level(l, lev):
                        if l == 0 and lev == 1:
                            act.wait_ge(sem("conv_done"), 4)
                        for half in range(2 if lev else 0):
                            name = f"t1_{l}_{lev}_{half}"
                            b = pr.filled(act, name)
                            L.free(f(T1[:, 3 * half:3 * half + 3, :], b[:, 0:T].rearrange("p (i q) -> p i q", i=3),
                                     ACT.Copy), pr, name, hold=False)

                    def own_head(b):
                        return b[:, 0:384].rearrange("p (h x) -> p h x", h=2)[:, :, 0:HD]

                    def solve(l, n_, step):
                        t = TILE_ORDER[LANES[l][0]][n_]
                        if step != "out":
                            dst, name = (rhs, "rhs") if step == "rhs" else (SA, "sa")
                            b = pr.filled(act, f"{name}{l}_{t}")
                            L.free(f(dst.rearrange("p (h v) -> p h v", h=2), own_head(b), ACT.Copy), pr, f"{name}{l}_{t}",
                                   hold=False)

                    def attention_inputs(k):
                        if k == 1:
                            b = pr.filled(act, "vtok")
                            L.free(f(Vt[:, 0:3, :], b[:, 0:T].rearrange("p (t q) -> p t q", t=3), ACT.Copy), pr, "vtok",
                                   hold=False)
                        for g in range(2 if k == 2 else 0):
                            b = pr.filled(act, f"kdup{g}")
                            L.step(f(Kd[g][0][HALF[0], :], b[HALF[0], :], ACT.Copy), hold=False)
                            L.free(f(Kd[g][1][HALF[1], :], b[HALF[1], :], ACT.Copy), pr, f"kdup{g}", hold=False)

                    def att_scores(u):
                        q, g, hs = UNITS[u]
                        nk = len(keys(q)) * P
                        act.wait_ge(sem("negm_ready"), u + 1)
                        for i in range(len(hs)):
                            name = f"s{u}_{i % 2}"
                            off = (i // 2) * P
                            src = bank[pr.place[name][0]][:, off:off + nk]
                            ins = f(Pm[:, i * nk:(i + 1) * nk], src, ACT.Exp, bias=negm[:, i:i + 1], scale=HD ** -0.5,
                                    accum_out=sums[:, i:i + 1])
                            if q == 0 and i < 2:
                                L.step(ins, hold=False)
                            else:
                                L.free(ins, pr, name, hold=False)
                        L.sig(f(esink[:, 0:len(hs)], esink[:, 0:len(hs)], ACT.Exp), "exps_ready", hold=False)

                    def att_turn(u):
                        n_ = 4 if UNITS[u][0] == 0 else 3
                        for i, name in enumerate([f"pt{u}_0", f"pt{u}_1"][:1 if n_ == 4 else 2]):
                            b = pr.filled(act, name)
                            L.free(f(PT[:, i * n_ * P:(i + 1) * n_ * P], b[:, 0:n_ * P], ACT.Copy), pr, name, hold=False)

                    steps = {"project": project, "front": front, "scores": lambda l: None, "level": level, "solve": solve,
                             "att_inputs": attention_inputs, "att_scores": att_scores, "att_scale": lambda u: None,
                             "att_turn": att_turn, "att_values": lambda u: None, "out_part": lambda part, j: None,
                             "mod_done": lambda: None, "short_conv": lambda: None, "shift_inputs": lambda d: None,
                             "mod_with": lambda k: None}
                    in_turn(lambda what, *which: steps[what](*which))

                    for c in range(2):
                        b = pr.filled(act, f"var{c}")
                        L.free(f((rn, A_)[c], b[:, 0:T], ACT.Sqrt, bias=ck("eps", 1, 1), scale=1.0 / HD), pr, f"var{c}",
                               hold=False)
                    for c in range(KC):
                        pr.copied(act, f"out1_{c}")
                        if c == 6:
                            pr.filled(act, "out1_7")
                        L.sig(f(sq[:, c, :], xT[:, c, :], ACT.Square), "sq_ready", hold=False)
                    norm(2)
                    modulate(2, (0, 1))
                    act.wait_ge(sem("gx_ready"), 1)
                    L.sig(f(gx, gx, ACT.Exp), "gexp_ready", hold=False)
                    for t in range(TILES):
                        for j in range(2):
                            b = pr.filled(act, f"htok{t}{j}")
                            L.free(f(h2tok[:, t, j * 512:(j + 1) * 512], b[:, :], ACT.Copy), pr, f"htok{t}{j}", hold=False)
                    act.wait_ge(sem("e21_ready"), 1)
                    L.sig(f(e21, e21, ACT.Exp), "e21exp_ready", hold=False)

                @block.vector
                def _(dve):
                    L = Lane(dve, "dve_steps")
                    v = nc.vector
                    tt, ts, stt = v.tensor_tensor, v.tensor_scalar, v.scalar_tensor_tensor

                    def wide(x, n):
                        return x[:, :, None].to_broadcast([P, x.shape[1], n])

                    add_experts(lambda ins: L.sig(ins, "residual_ready", hold=False))

                    def mod_part_copy(n):
                        b = pr.filled(dve, f"mod{n}")
                        L.free(v.tensor_copy(mod_part[n % 2], b[:, 0:UC]), pr, f"mod{n}", hold=False)

                    def mod_add(name, lo, hi):
                        b = pr.filled(dve, name)
                        L.free(tt(mod[:, lo:hi, :], b[:, 2 * lo:2 * hi].rearrange("p (j s) -> p j s", s=2),
                                  wide(pk("b_mod", lo, hi - lo), 2), ALU.add), pr, name)

                    def gains_of(n, first, name):
                        L.sig(stt(gain[:, n, :, :], mod[:, first:first + 8, :], 1.0, wide(pk(name, 0, 8), 2),
                                   ALU.add, ALU.mult), "gain_ready")

                    def reciprocal_root(n):
                        pr.copied(dve, f"ss{n}")
                        L.step(v.reciprocal(rstd, ss))

                    def modulate_sample():
                        cols, pad = STREAMS[1]
                        for c in range(KC):
                            L.sig(ts(hT[:, c, pad], n1[:, c, cols], gain[:, 0, c, 1:2], mod[:, c, 1:2], ALU.mult, ALU.add),
                                  "h_sample_ready", hold=False)

                    for n in range(N_MOD1):
                        mod_part_copy(n)
                        if n == 5:
                            reciprocal_root(1)
                        if n >= 6:
                            half = slice((n - 6) * 4, (n - 5) * 4)
                            L.sig(tt(n1[:, half, :], xT[:, half, :], rstd[:, None, :].to_broadcast([P, 4, T]), ALU.mult),
                                  "n_ready", hold=n == 7)
                    dve.wait_ge(sem("small_loaded"), 16 * 7)
                    L.step(ts(negmu, pk("mu", 8, 8), -1.0, None, ALU.mult), hold=False)
                    L.step(ts(omka, pk("ka", 0, 4), -1.0, 1.0, ALU.mult, ALU.add), hold=False)
                    mod_add("mod_first", 0, 16)
                    gains_of(0, 8, "norm_mix")
                    modulate_sample()
                    for h in range(2):
                        for x in (lora[h], BK[0][h], BK[1][h]):
                            L.step(v.memset(x[HALF[1 - h], :], 0.0), hold=False)
                    for k in range(5):
                        for m in MOD_WITH[k]:
                            mod_part_copy(m)
                    for i in range(12, 20):
                        pr.copied(dve, f"in{i}")
                    L.step(tt(diff, slab[:, :, 0:W - 1], slab[:, :, 1:W], ALU.subtract))

                    def shifted(dst, d, j, name=None):
                        for n, (cols, pad) in enumerate(STREAMS):
                            behind = slice(pad.start - 1 + d, pad.stop - 1 + d)
                            mu = negmu[:, j:j + 1] if d else pk("mu", j)
                            ins = stt(dst[:, cols], diff[:, j, behind], mu, slab[:, j, pad], ALU.mult, ALU.add)
                            if n and name:
                                L.sig(ins, name, hold=False)
                            else:
                                L.step(ins, hold=False)

                    def z_inputs(d):
                        if d:
                            pr.filled(dve, "lora1_0")
                        shifted(Z[:, 0, :], d, 6)
                        shifted(Z[:, 1, :], d, 7, "z_ready")

                    def tiles3(x):
                        return x.rearrange("p (t q) -> p t q", t=TILES)

                    def front(l, k):
                        d, c = LANES[l]
                        i, q = 2 * d + c, l % 2
                        if k == 0:
                            if l:
                                dve.wait_ge(sem("padded_ready"), l)
                                pr.filled(dve, f"tokk{l - 1}")
                            shifted(K_, d, 2 + c, "kv_ready")
                            if l:
                                pr.filled(dve, f"tokv{l - 1}")
                            shifted(V_, d, 4 + c, "v_ready")
                        elif k == 1:
                            shifted(R_, d, c)
                            pr.copied(dve, f"decay{l}")
                            if l:
                                dve.wait_ge(sem("exp_ready"), l)
                            L.step(v.tensor_tensor_scan(Lp, ck("reset", 3 * 129), Sg, 0.0, ALU.mult, ALU.add))
                            L.step(v.tensor_copy(cmid, tiles3(Lp)[:, :, 64]))
                            L.sig(tt(tiles3(Lp), tiles3(Lp), wide(cmid, 129), ALU.subtract), "sums_ready", hold=False)
                        elif k == 2:
                            pr.copied(dve, f"rate{l}")
                            if l:
                                pr.filled(dve, f"bon{l - 1}")
                            L.step(ts(t2, A_, pk("ka", i), omka[:, i:i + 1], ALU.mult, ALU.add))
                        elif k == 4:
                            pr.copied(dve, f"norm{l}")
                            L.step(ts(rn, rn, 1e-12, None, ALU.max))
                            L.step(v.reciprocal(rn[:, 0:T // 2], rn[:, 0:T // 2]), hold=False)
                        elif k == 5:
                            L.step(v.reciprocal(rn[:, T // 2:T], rn[:, T // 2:T]))
                            L.step(stt(kkn, K_, pk("kk", i), rn, ALU.mult, ALU.mult), hold=False)
                        elif k == 6:
                            dve.wait_ge(L.s, L.n)
                            L.step(tt(rn, kkn, A_, ALU.mult), hold=False)
                            L.step(tt(K_, K_, t2, ALU.mult))
                            L.sig(stt(t2, R_, pk("rk", i), K_, ALU.mult, ALU.mult), "rk_ready", hold=False)
                        elif k == 7:
                            dve.wait_ge(L.s, L.n)
                            dve.wait_ge(sem("exp_ready"), l + 1)
                            E3, M3 = tiles3(Ep), tiles3(Em)
                            if d == 0:
                                ea, er, eb = E3[:, :, 0:P], E3[:, :, 1:1 + P], M3[:, :, 1:1 + P]
                                e_mid, e_end = M3[:, :, 0], E3[:, :, P]
                            else:
                                ea, er, eb = M3[:, :, 1:1 + P], M3[:, :, 0:P], E3[:, :, 0:P]
                                e_mid, e_end = E3[:, :, P], M3[:, :, 0]
                            L.step(v.tensor_copy(ec[:, l, 0, :], e_mid), hold=False)
                            L.step(v.tensor_copy(ec[:, l, 1, :], e_end), hold=False)
                            L.step(stt(AR[q][:, :, 0, :], tiles3(kkn), -1.0, ea, ALU.mult, ALU.mult), hold=False)
                            L.step(tt(AR[q][:, :, 1, :], tiles3(R_), er, ALU.mult), hold=False)
                            L.step(tt(tiles3(rn), tiles3(rn), eb, ALU.mult), hold=False)
                            L.sig(tt(tiles3(K_), tiles3(K_), eb, ALU.mult), "decayed_ready")
                        elif k == 8:
                            b = pr.filled(dve, f"bon{l}")
                            if d == 0:
                                L.free(tt(bonus[:, c, :], b[:, 0:T], V_, ALU.mult), pr, f"bon{l}", hold=False)
                            else:
                                L.free(tt(t2, b[:, 0:T], V_, ALU.mult), pr, f"bon{l}")
                                L.step(tt(bonus[:, c, :], bonus[:, c, :], t2, ALU.add), hold=False)

                    def scores(l):
                        d = LANES[l][0]
                        m = ck("tri", 2 * P, 2 * P * d)[:, None, :].to_broadcast([P, 2, 2 * P])
                        for t in range(TILES):
                            for h in range(2):
                                b = pr.filled(dve, f"g{l}_{t}_{h}")
                                L.free(tt(G[:, t, h, :, :, :].rearrange("p w a q -> p w (a q)"),
                                          b[:, :].rearrange("p (w q) -> p w q", w=2), m, ALU.mult),
                                       pr, f"g{l}_{t}_{h}", hold=False)

                    def level(l, lev):
                        eye = ident[:, None, :].to_broadcast([P, 3, P])
                        if lev == 0:
                            dve.wait_ge(sem("level_ready"), l * LEVELS + 1)
                        for half in range(2):
                            ii = slice(3 * half, 3 * half + 3)
                            if lev == 0:
                                name = f"t1_{l}_0_{half}"
                                b = pr.filled(dve, name)
                                L.free(tt(X_[:, ii, :], b[:, 0:T].rearrange("p (i q) -> p i q", i=3), eye, ALU.add),
                                       pr, name, hold=False)
                                L.sig(tt(XT[:, ii, :], Nl[0][:, ii, :], eye, ALU.add), "x_ready", hold=False)
                                continue
                            for what, x in (("dx", X_), ("dxt", XT)):
                                if what == "dx" and lev == LEVELS - 1:
                                    continue
                                name = f"{what}_{l}_{lev}_{half}"
                                b = pr.filled(dve, name)
                                L.free(tt(x[:, ii, :], x[:, ii, :], b[:, 0:T].rearrange("p (i q) -> p i q", i=3),
                                          ALU.add), pr, name, hold=False)

                    def solve(l, n_, step):
                        d, c = LANES[l]
                        order = TILE_ORDER[d]
                        t = order[n_]
                        if step == "sa":
                            return
                        if step == "rhs" and n_:
                            return
                        if step == "rhs":
                            for h in range(2):
                                ins = ts(S0c[HALF[h], HALF[h]], S0[HALF[h], l, :],
                                         ec[HALF[h], l, 0, order[1]:order[1] + 1], None, ALU.mult)
                                if h:
                                    L.sig(ins, "seed_ready")
                                else:
                                    L.step(ins, hold=False)
                            return
                        if n_ < 2:
                            b = pr.filled(dve, f"state{l}_{t}")
                            end = ec[:, l, 1, t:t + 1]
                            if n_ == 0:
                                L.free(ts(Sout[:, l, :], b[:, 0:HD], end, None, ALU.mult), pr, f"state{l}_{t}",
                                       hold=False)
                            else:
                                L.step(tt(stmp[HALF[0], :], b[HALF[0], 0:HD], S0c[HALF[0], HALF[0]], ALU.add), hold=False)
                                L.free(tt(stmp[HALF[1], :], b[HALF[1], 0:HD], S0c[HALF[1], HALF[1]], ALU.add), pr,
                                       f"state{l}_{t}")
                        b = pr.filled(dve, f"y{l}_{t}")
                        dst = ys[:, c, t * P:(t + 1) * P]
                        if d == 0:
                            L.free(v.tensor_copy(dst, b[:, 0:P]), pr, f"y{l}_{t}", hold=False)
                        else:
                            L.free(tt(dst, dst, b[:, 0:P], ALU.add), pr, f"y{l}_{t}", hold=False)
                        if n_ == 1:
                            nt = order[2]
                            for h in range(2):
                                ins = ts(S0c[HALF[h], HALF[h]], stmp[HALF[h], :], ec[HALF[h], l, 1, t:t + 1],
                                         ec[HALF[h], l, 0, nt:nt + 1], ALU.mult, ALU.mult)
                                if h:
                                    L.sig(ins, "seed_ready")
                                else:
                                    L.step(ins, hold=False)

                    def short_conv():
                        for i in range(6):
                            pr.copied(dve, f"in{i}")
                        L.step(tt(conv[:, 2:4, :], conv[:, 2:4, :], conv[:, 4:6, :], ALU.mult))
                        for c in range(2):
                            u, acc = conv[:, 2 + c, :], conv[:, 4 + c, 1:W - 1]
                            L.step(ts(acc, u[:, 0:W - 2], pk("conv_w", c), None, ALU.mult))
                            L.step(stt(acc, u[:, 1:W - 1], pk("conv_w", 2 + c), acc, ALU.mult, ALU.add))
                            L.step(stt(acc, u[:, 2:W], pk("conv_w", 4 + c), acc, ALU.mult, ALU.add))
                            for cols, pad in STREAMS:
                                L.sig(tt(mixT[:, c, cols], conv[:, 4 + c, pad], conv[:, c, pad], ALU.mult), "conv_done",
                                      hold=False)

                    def attention_inputs(k):
                        if k:
                            return
                        cos, sin = ck("cos", TS), ck("sin", TS)
                        b = pr.filled(dve, "swapk")
                        for g in range(2):
                            for h in range(2):
                                ins = v.memset(Kd[g][h][HALF[1 - h], :], 0.0)
                                if g and h:
                                    L.sig(ins, "kd_zero", hold=False)
                                else:
                                    L.step(ins, hold=False)
                        L.free(tt(rtmp[:, 0:TS], b[:, 0:TS], sin, ALU.mult), pr, "swapk", hold=False)
                        L.step(tt(kT[:, TP:T], kraw, cos, ALU.mult))
                        L.sig(tt(kT[:, TP:T], kT[:, TP:T], rtmp[:, 0:TS], ALU.add), "k_roped")
                        for j in range(2):
                            b = pr.filled(dve, f"swapq{j}")
                            r2 = rtmp.rearrange("p (j c t) -> p j c t", j=2, c=2)[:, j]
                            q2 = qT[:, 2 * j:2 * j + 2, TP:T]
                            L.free(tt(r2, b[:, :].rearrange("p (c t) -> p c t", c=2),
                                      sin[:, None, :].to_broadcast([P, 2, TS]), ALU.mult), pr, f"swapq{j}", hold=False)
                            L.step(tt(q2, q2, cos[:, None, :].to_broadcast([P, 2, TS]), ALU.mult))
                            L.sig(tt(q2, q2, r2, ALU.add), "q_roped", hold=False)

                    def att_scores(u):
                        q, g, hs = UNITS[u]
                        nh = len(hs)
                        sink = pk("sink", 4 * g + hs[0], nh)
                        m_, n_, e_ = mx[:, 0:nh], negm[:, 0:nh], esink[:, 0:nh]
                        for i in range(2):
                            b = pr.filled(dve, f"s{u}_{i}")
                            if q == 0:
                                L.step(v.reduce_max(mx.rearrange("p (c h) -> p h c", h=2)[:, i, :],
                                                    b[:, 0:2 * P].rearrange("p (c k) -> p c k", c=2), AX.X), hold=i == 1)
                            else:
                                L.step(v.reduce_max(mx[:, i:i + 1], b[:, 0:3 * P], AX.X), hold=i == 1)
                        L.step(stt(m_, m_, HD ** -0.5, sink, ALU.mult, ALU.max))
                        L.step(ts(n_, m_, -1.0, None, ALU.mult))
                        L.sig(tt(e_, sink, n_, ALU.add), "negm_ready")

                    def att_scale(u):
                        q, g, hs = UNITS[u]
                        nh, nk = len(hs), len(keys(q)) * P
                        dve.wait_ge(sem("exps_ready"), u + 1)
                        L.step(tt(rden[:, 0:nh], sums[:, 0:nh], esink[:, 0:nh], ALU.add))
                        L.step(v.reciprocal(rden[:, 0:nh], rden[:, 0:nh]))
                        for i in range(nh):
                            ins = ts(Pm[:, i * nk:(i + 1) * nk], Pm[:, i * nk:(i + 1) * nk], rden[:, i:i + 1], None, ALU.mult)
                            if i < nh - 1:
                                L.step(ins, hold=False)
                            else:
                                L.sig(ins, "p_ready", hold=False)

                    def att_values(u):
                        q, g, hs = UNITS[u]
                        nh = len(hs)
                        b = pr.filled(dve, f"o{u}")
                        c0, n_ = 2 + 2 * g + hs[0] // 2, nh // 2
                        L.free(v.tensor_copy(mixT[:, c0:c0 + n_, q * P:(q + 1) * P],
                                             b[:, 0:n_ * P].rearrange("p (c q) -> p c q", c=n_)), pr, f"o{u}", hold=False)

                    def mod_done():
                        mod_add("mod_rest", 16, 48)
                        gains_of(1, 32, "norm_ffn")

                    def out_part(part, j):
                        b = pr.filled(dve, f"out{part}_{j}")
                        for st, (cols, _) in enumerate(STREAMS):
                            ins = stt(xT[:, j, cols], b[:, cols], mod[:, 16 + j, st:st + 1], xT[:, j, cols],
                                      ALU.mult, ALU.add)
                            if st:
                                L.free(ins, pr, f"out{part}_{j}", hold=False)
                            else:
                                L.step(ins, hold=False)

                    z_inputs(0)
                    steps = {"project": lambda u, j: None, "front": front, "scores": scores, "level": level,
                             "solve": solve, "att_inputs": attention_inputs, "att_scores": att_scores,
                             "att_scale": att_scale, "att_turn": lambda u: None, "att_values": att_values,
                             "out_part": out_part, "mod_done": mod_done, "short_conv": short_conv,
                             "shift_inputs": z_inputs,
                             "mod_with": lambda k: [mod_part_copy(m) for m in MOD_WITH[k]]}
                    in_turn(lambda what, *which: steps[what](*which))

                    for c in range(2):
                        b = pr.filled(dve, f"mean{c}")
                        L.free(stt(ys[:, c, :], b[:, 0:T], -1.0 / HD, ys[:, c, :], ALU.mult, ALU.add), pr, f"mean{c}")
                        L.sig(tt(Z[:, c, :], ys[:, c, :], ys[:, c, :], ALU.mult), "ysq_ready", hold=False)
                    for c in range(2):
                        y, r = ys[:, c, :], (rn, A_)[c]
                        pr.copied(dve, f"var{c}")
                        L.step(v.reciprocal(r, r))
                        L.step(tt(y, y, r, ALU.mult))
                        L.step(ts(y, y, pk("ln_g", c), pk("ln_b", c), ALU.mult, ALU.add))
                        L.step(tt(y, y, bonus[:, c, :], ALU.add))
                        L.sig(tt(mixT[:, 6 + c, :], y, gate[:, c, :], ALU.mult), "mix_ready", hold=False)

                    out_part(0, 6)
                    out_part(0, 7)
                    for j in range(KC):
                        out_part(1, j)
                    L.sig(v.memset(zeros, 0.0), "zero_ready", hold=False)
                    reciprocal_root(2)
                    for c in range(KC):
                        L.sig(tt(n1[:, c, :], xT[:, c, :], rstd, ALU.mult), "n_ready", hold=False)

                    def first_best(out, x, m, n, rev):
                        L.step(v.reduce_max(m, x, AX.X))
                        L.step(tt(out, x, wide(m, n), ALU.is_equal))
                        L.step(tt(out, out, rev[:, None, :].to_broadcast([P, TILES, n]), ALU.mult))
                        L.step(v.reduce_max(gs, out, AX.X))
                        L.step(tt(out, out, wide(gs, n), ALU.is_equal))

                    b = pr.filled(dve, "route")
                    L.free(tt(lg, b[:, 0:TILES * 36].rearrange("p (t e) -> p t e", t=TILES),
                              pk("rt_b", 0, 36)[:, None, :].to_broadcast([P, TILES, 36]), ALU.add), pr, "route")
                    first_best(goh, lg[:, :, 0:4], gm, 4, ck("rev", 4, 4))
                    L.sig(tt(gx, lg[:, :, 0:4], wide(gm, 4), ALU.subtract), "gx_ready")
                    lge = lg[:, :, 4:36].rearrange("p t (g e) -> p t g e", g=N_GROUPS)
                    for t in range(TILES):
                        L.step(tt(el4[:, t, :, :], lge[:, t, :, :], wide(goh[:, t, :], EPG), ALU.mult), hold=t == TILES - 1)
                    L.step(v.reduce_sum(el, el4.rearrange("p t g e -> p t e g"), AX.X))
                    first_best(oh1, el, m1, EPG, ck("rev", EPG))
                    L.step(stt(el, oh1, -3e38, el, ALU.mult, ALU.add))
                    first_best(oh2, el, m2, EPG, ck("rev", EPG))
                    L.sig(tt(e21, m2, m1, ALU.subtract), "e21_ready")
                    dve.wait_ge(sem("gexp_ready"), 1)
                    L.step(v.reduce_sum(gs, gx, AX.X))
                    dve.wait_ge(sem("e21exp_ready"), 1)
                    L.step(ts(w1_, e21, 1.0, None, ALU.add))
                    L.step(tt(w1_, w1_, gs, ALU.mult))
                    L.step(v.reciprocal(w1_, w1_))
                    L.step(tt(w2_, w1_, e21, ALU.mult))
                    L.step(tt(tw, oh1, wide(w1_, EPG), ALU.mult), hold=False)
                    L.step(tt(el, oh2, wide(w2_, EPG), ALU.mult))
                    L.step(tt(tw, tw, el, ALU.add), hold=False)
                    L.step(tt(oh1, oh1, oh2, ALU.add))
                    for t in range(TILES):
                        e8 = oh1[:, t, None, :].to_broadcast([P, N_GROUPS, EPG])
                        w8 = tw[:, t, None, :].to_broadcast([P, N_GROUPS, EPG])
                        g8 = wide(goh[:, t, :], EPG)
                        L.step(tt(wall3[:, t, :].rearrange("p (g e) -> p g e", g=N_GROUPS), g8, w8, ALU.mult), hold=False)
                        ins = tt(asg[:, t, :, :], g8, e8, ALU.mult)
                        if t < TILES - 1:
                            L.step(ins, hold=False)
                        else:
                            L.sig(ins, "asg_ready")
                    b = pr.filled(dve, "pos")
                    flat = asg.rearrange("p t g e -> p (t g e)")
                    L.step(stt(posm[:, :], b[:, 0:TILES * N_EXP], 1.0, flat, ALU.add, ALU.mult))
                    L.step(ts(posm[:, :], posm[:, :], -1.0, None, ALU.add), hold=False)
                    L.free(v.reduce_max(rnd[:, 7:8], b[:, T:T + N_EXP], AX.X), pr, "pos")
                    for k in range(1, MAX_ROUNDS):
                        L.step(ts(rnd[:, k:k + 1], rnd[:, 7:8], float(k * SLOTS), None, ALU.is_gt), hold=k == MAX_ROUNDS - 1)
                    L.step(v.reduce_sum(rnd[:, 0:1], rnd[:, 1:MAX_ROUNDS], AX.X))
                    L.step(ts(rounds_i[:, :], rnd[:, 0:1], 1.0, None, ALU.add))

        PAIRS = N_EXP // 2

        def experts_round(layer):
            IN_PAIR = 4
            A_UP, A_WT, A_TOK, A_DOWN = 1, 2, 3, 4
            B_UP, B_HT, B_DOWN, B_TOK = 1, 2, 3, 4
            LAST = PAIRS - 1
            bA, bB = bank[6], bank[7]
            js = "p j s -> p (j s)"

            with nc.Block() as block:
                def full_a(eng, i, k):
                    eng.wait_ge(sem("a_filled"), i * IN_PAIR + (k + 1))

                def full_b(eng, i, k):
                    eng.wait_ge(sem("b_filled"), i * IN_PAIR + (k + 1))

                def emptied_a(eng, i, k):
                    eng.wait_ge(sem("a_emptied"), i * IN_PAIR + (k + 1))

                def emptied_b(eng, i, k):
                    eng.wait_ge(sem("b_emptied"), i * IN_PAIR + (k + 1))

                def pairs(eng, body):
                    with eng.Fori(0, LAST) as i:
                        body(i, False)
                    body(LAST, True)

                @block.sync
                def _(sp):
                    def load(i, m, j):
                        name, rows = (("exp_w1", D), ("exp_w3", D), ("exp_w2", DE))[m]
                        src = a[name][bass.ds((layer * N_EXP + i * 2 + j) * rows, rows), :]
                        sp.dma_start(unit[2 * m + j].rearrange("p (c n) -> p c n", c=rows // P),
                                     src.rearrange("(c p) n -> p c n", p=P)).then_inc(sem(f"unit{2 * m + j}"), 16)

                    for m, j in ((1, 1), (2, 0), (2, 1)):
                        load(0, m, j)
                    with sp.Fori(1, PAIRS) as i:
                        for m in range(3):
                            if m == 0:
                                full_a(sp, i - 1, A_UP)
                            else:
                                full_b(sp, i - 1, B_UP if m == 1 else B_DOWN)
                            for j in range(2):
                                load(i, m, j)
                    full_a(sp, LAST, A_UP)
                    for j in range(2):
                        load(0, 0, j)
                    full_b(sp, LAST, B_UP)
                    load(0, 1, 0)
                    for u in range(3):
                        sp.wait_ge(sem(f"unit{u}"), 16 * PAIRS)

                @block.tensor
                def _(pe):
                    mm = nc.tensor.matmul

                    def gather(half):
                        b = bB if half else bA
                        for c in range(4):
                            for t in range(TILES):
                                last = mm(b[:, c * P:(c + 1) * P], h2tok[:, t, (4 * half + c) * P:(4 * half + c + 1) * P],
                                          Sel[:, t, :, :].rearrange(js), start=(t == 0), stop=(t == TILES - 1))
                        last.then_inc(sem("b_filled" if half else "a_filled"), 1)

                    def loaded(i, m, j):
                        if 2 * m + j > 2:
                            pe.wait_ge(sem(f"unit{2 * m + j}"), i * 16 + 16)
                        elif not (isinstance(i, int) and i == 0):
                            pe.wait_ge(sem(f"unit{2 * m + j}"), i * 16)

                    def up(i):
                        emptied_a(pe, i, 0)
                        for m, b in ((0, bA), (1, bB)):
                            for j in range(2):
                                loaded(i, m, j)
                            if m:
                                emptied_b(pe, i, 0)
                            for c in range(KC):
                                if c == 4 and not m:
                                    emptied_b(pe, i, 0)
                                for j in range(2):
                                    last = mm(b[HALF[j], :], Xg[:, c, j, :], unit[2 * m + j][:, c * DE:(c + 1) * DE],
                                              start=(c == 0), stop=(c == KC - 1))
                            last.then_inc(sem("b_filled" if m else "a_filled"), 1)

                    def scatter():
                        for c in range(KC):
                            for bk, col, t0, n in segments(c):
                                mm(bank[bk][:, col:col + n], yg[:, c * P:(c + 1) * P], WselT[:, t0:t0 + n],
                                   start=False, stop=True, skip_group_check=True)

                    def down(i, half, last_pair):
                        b = bB if half else bA
                        for f_ in range(FC):
                            for j in range(2):
                                lo = f_ * D + half * 512
                                last = mm(b[HALF[j], :], hidT[:, f_, j, :], unit[4 + j][:, lo:lo + 512],
                                          start=(f_ == 0), stop=(f_ == FC - 1))
                        last.then_inc(sem("b_filled" if half else "a_filled"), 1)

                    def rest(i, last_pair):
                        pe.wait_ge(sem("wsel_ready"), i + 1)
                        emptied_a(pe, i, A_UP)
                        for t in range(TILES):
                            last = nc.tensor.transpose(bA[:, t * P:(t + 1) * P], Wsel[:, t, :, :].rearrange(js), ident)
                        last.then_inc(sem("a_filled"), 1)
                        emptied_b(pe, i, B_UP)
                        for f_ in range(FC):
                            last = nc.tensor.transpose(bB[:, f_ * P:(f_ + 1) * P], hid[:, f_ * P:(f_ + 1) * P], ident)
                        last.then_inc(sem("b_filled"), 1)
                        emptied_a(pe, i, A_WT)
                        if not last_pair:
                            pe.wait_ge(sem("sel_ready"), i + 2)
                            gather(0)
                        for j in range(2):
                            loaded(i, 2, j)
                        emptied_b(pe, i, B_HT)
                        if not last_pair:
                            emptied_a(pe, i, A_TOK)
                        down(i, 0, last_pair)
                        down(i, 1, last_pair)
                        if not last_pair:
                            emptied_b(pe, i, B_DOWN)
                            gather(1)

                    pe.wait_ge(sem("sel_ready"), 1)
                    gather(0)
                    gather(1)
                    up(0)
                    rest(0, False)
                    with pe.Fori(1, LAST) as i:
                        up(i)
                        scatter()
                        rest(i, False)
                    up(LAST)
                    scatter()
                    rest(LAST, True)
                    emptied_a(pe, LAST, A_DOWN - 1)
                    emptied_b(pe, LAST, B_DOWN)
                    scatter()

                @block.vector
                def _(dve):
                    v = nc.vector

                    def select(i):
                        pair = bass.ds(i * 2, 2)
                        iota = ck("iota", SLOTS)[:, None, :].to_broadcast([P, 2, SLOTS])
                        for t in range(TILES):
                            ins = v.tensor_tensor(Sel[:, t, :, :], iota,
                                                  pos3[:, t, pair][:, :, None].to_broadcast([P, 2, SLOTS]), ALU.is_equal)
                        ins.then_inc(sem("sel_ready"), 1)
                        dve.wait_ge(sem("sel_ready"), i + 1)

                    def tokens(i, k):
                        full_b(dve, i, k)
                        v.tensor_copy(Xg[:, 4:8, :, :].rearrange("p c j s -> p c (j s)"),
                                      bB[:, :].rearrange("p (c s) -> p c s", c=4)).then_inc(sem("b_emptied"), 1)

                    def body(i, last_pair):
                        pair = bass.ds(i * 2, 2)
                        for t in range(TILES):
                            ins = v.tensor_tensor(Wsel[:, t, :, :], Sel[:, t, :, :],
                                                  wall3[:, t, pair][:, :, None].to_broadcast([P, 2, SLOTS]), ALU.mult)
                        ins.then_inc(sem("wsel_ready"), 1)
                        if not last_pair:
                            dve.wait_ge(sem("wsel_ready"), i + 1)
                            select(i + 1)
                        full_b(dve, i, B_UP)
                        emptied_a(dve, i, A_UP)
                        v.tensor_tensor(hid, sil, bB[:, :], ALU.mult).then_inc(sem("b_emptied"), 1)
                        full_b(dve, i, B_HT)
                        v.tensor_copy(hidT.rearrange("p f j s -> p (f j s)"), bB[:, :]).then_inc(sem("b_emptied"), 1)
                        full_b(dve, i, B_DOWN)
                        v.tensor_copy(yg[:, 512:], bB[:, :]).then_inc(sem("b_emptied"), 1)
                        if not last_pair:
                            tokens(i, B_TOK)

                    select(0)
                    tokens(0, 0)
                    pairs(dve, body)
                    v.tensor_scalar(posm[:, :], posm[:, :], float(-SLOTS), None, ALU.add).then_inc(sem("pos_moved"), 1)

                @block.scalar
                def _(act):
                    f = nc.scalar.activation

                    def tokens(i, k):
                        full_a(act, i, k)
                        f(Xg[:, 0:4, :, :].rearrange("p c j s -> p c (j s)"),
                          bA[:, :].rearrange("p (c s) -> p c s", c=4), ACT.Copy).then_inc(sem("a_emptied"), 1)

                    def body(i, last_pair):
                        full_a(act, i, A_UP)
                        f(sil, bA[:, :], ACT.Silu).then_inc(sem("a_emptied"), 1)
                        full_a(act, i, A_WT)
                        f(WselT, bA[:, 0:T], ACT.Copy).then_inc(sem("a_emptied"), 1)
                        if not last_pair:
                            tokens(i, A_TOK)
                        full_a(act, i, A_DOWN - 1 if last_pair else A_DOWN)
                        f(yg[:, 0:512], bA[:, :], ACT.Copy).then_inc(sem("a_emptied"), 1)

                    tokens(0, 0)
                    pairs(act, body)

        def close_sums():
            with nc.Block() as block:
                @block.vector
                def _(dve):
                    add_experts()

        def final_stage():
            with nc.Block() as block:
                @block.scalar
                def _(act):
                    f = nc.scalar.activation
                    f(sq[:, :, :], xT[:, :, :], ACT.Square).then_inc(sem("sq_ready"), 1)
                    act.wait_ge(sem("ss_filled"), 1)
                    f(ss[:, :], bank[0][:, 0:T], ACT.Sqrt, bias=ck("eps", 1), scale=1.0 / D).then_inc(sem("std_ready"), 1)

                @block.tensor
                def _(pe):
                    pe.wait_ge(sem("sq_ready"), 1)
                    for c in range(KC):
                        last = nc.tensor.matmul(bank[0][:, 0:T], ones, sq[:, c, :], start=(c == 0), stop=(c == KC - 1))
                    last.then_inc(sem("ss_filled"), 1)

                @block.vector
                def _(dve):
                    dve.wait_ge(sem("std_ready"), 1)
                    nc.vector.reciprocal(rstd, ss).then_inc(sem("rstd_ready"), 1)
                    dve.wait_ge(sem("rstd_ready"), 1)
                    for c in range(KC):
                        nc.vector.scalar_tensor_tensor(h2T[:, c, :], xT[:, c, :], nout[:, c:c + 1], rstd,
                                                       ALU.mult, ALU.mult).then_inc(sem("y_ready"), 1)

                @block.sync
                def _(sp):
                    sp.wait_ge(sem("y_ready"), KC)
                    sp.dma_start(o["yT"], h2T.rearrange("p c t -> p (c t)")).then_inc(sem("stored"), 16)
                    sp.wait_ge(sem("stored"), 16)

        with nc.Block() as block:
            s_const, s_cond = sem("const_loaded"), sem("cond_loaded")

            @block.sync
            def _(sp):
                sp.dma_start(x_sb[:, :], a["xT"]).then_inc(s_const, 16)
                sp.dma_start(const[:, :], a["const"]).then_inc(s_const, 16)
                sp.dma_start(nout[:, :], a["nout"]).then_inc(s_const, 16)
                sp.wait_ge(s_const, 48)

            @block.scalar
            def _(act):
                act.dma_start(cond[:, :], a["cond"]).then_inc(s_cond, 16)
                act.wait_ge(s_cond, 16)

            @block.vector
            def _(dve):
                nc.vector.memset(mod_sb[:, :], 0.0)
                nc.vector.memset(zeros, 0.0).then_inc(sem("sums_cleared"), 1)

            @block.tensor
            def _(pe):
                pe.wait_ge(sem("sums_cleared"), 1)
                for b in range(SUM_BANKS):
                    nc.tensor.matmul(bank[b][:, :], zeros[:, 0:P], zeros[:, 0:512], start=True, stop=True)

        with nc.Fori(0, DEPTH) as layer:
            mixer_stage(layer)
            clear(list(sems.values()))
            n_rounds = nc.values_load(rounds_i[0:1, 0:1], min_val=1, max_val=MAX_ROUNDS)
            with nc.Fori(0, n_rounds):
                experts_round(layer)
                clear(list(sems.values()))
        close_sums()
        final_stage()


def constants():
    i = np.arange(P)
    s, t = i[:, None], i[None, :]
    out = np.zeros((P, NCK), np.float32)

    def put(name, x, off=0):
        out[:, CK[name] + off:CK[name] + off + x.shape[1]] = x

    put("ident", s == t)
    put("ones", np.ones((P, P)))
    put("heads", s // HD == t // HD)
    put("before", s < t)
    put("swap", np.where((t % 32 < 16) & (s == t + 16), -1.0, np.where((t % 32 >= 16) & (s == t - 16), 1.0, 0.0)))
    put("pick", np.where((np.arange(2 * P - 2)[None, :] >= P - 2) & (np.arange(2 * P - 2)[None, :] < P)
                         & (s % 32 == np.arange(2 * P - 2)[None, :] - (P - 2)), 1.0, 0.0))
    inv = np.float32(10000.0) ** (-np.arange(0, 32, 2, dtype=np.float32) / np.float32(32))
    tok = np.arange(TS)
    pos = np.where((i % HD < 32)[:, None], (tok // 64)[None, :], (tok % 64)[None, :]).astype(np.float32)
    ang = pos * inv[i % 16][:, None].astype(np.float32)
    put("cos", np.cos(ang))
    put("sin", np.sin(ang))
    put("att", np.where(t > s, -1e30, 0.0))
    put("att", np.where(t < s, -1e30, 0.0), P)
    for n, m in enumerate((s < t, s <= t, s > t, s >= t)):
        put("tri", m, n * P)
    for lev in range(LEVELS):
        put("level", ((t >> lev) & 1 == 1) & (s >> lev == (t >> lev) - 1), lev * P)
        put("level", ((t >> lev) & 1 == 0) & (s >> lev == (t >> lev) + 1), (LEVELS + lev) * P)
    put("reset", np.tile((np.arange(3 * 129) % 129 != 0)[None, :], (P, 1)))
    put("iota", np.tile(np.arange(SLOTS)[None, :], (P, 1)))
    put("rev", np.tile(np.arange(EPG, 0, -1)[None, :], (P, 1)))
    put("eps", np.tile(np.array([[NORM_EPS, GN_EPS]]), (P, 1)))
    return out


def layouts(i):
    L = DEPTH
    cat = np.concatenate

    def chunks(x, n):
        return np.swapaxes(x.reshape(*x.shape[:-1], n, P), -1, -2)

    def rows(x):
        return np.ascontiguousarray(x.reshape(L * P, -1))

    x = cat([i["x_prompt"][0], i["x_sample"][0]], 0)
    cond = np.stack([i["c_ctx"], i["c"][0]], 0)
    per = []
    for l in range(L):
        def two(n):
            return chunks(i[n][l], 2).transpose(1, 0, 2).reshape(P, 4)
        per.append(cat([
            chunks(i["b_mod"][l], 48), chunks(i["norm_mix"][l], 8), chunks(i["norm_ffn"][l], 8),
            chunks(i["conv_w"][l], 2).transpose(1, 0, 2).reshape(P, 6),
            chunks(i["rw_mu"][l], 8).transpose(1, 0, 2).reshape(P, 16),
            two("rw_w0"), two("rw_a0"), two("rw_kk"), two("rw_ka"), two("rw_rk"),
            chunks(i["rw_ln_g"][l], 2), chunks(i["rw_ln_b"][l], 2),
            np.broadcast_to(i["attn_sink"][l], (P, 8)),
            np.broadcast_to(cat([i["rt_group_b"][l], i["rt_exp_b"][l]]), (P, 36))], 1))
    w1a1 = cat([i["rw_w1"], i["rw_a1"]], -1).reshape(L, 2, 2, P, P).transpose(0, 3, 1, 2, 4)
    w2a2 = cat([i["rw_w2"], i["rw_a2"]], 2).transpose(0, 2, 1, 3)
    rtw = cat([i["rt_group_w"], i["rt_exp_w"]], -1).reshape(L, KC, P, 36).transpose(0, 2, 1, 3)
    s0 = i["state_wkv"][0].reshape(L, 2, 2, 2, HD, HD).transpose(0, 3, 5, 1, 2, 4)
    return {
        "xT": chunks(x, KC).transpose(1, 2, 0).reshape(P, KC * T),
        "cond": chunks(cond, KC).transpose(1, 2, 0).reshape(P, 2 * KC),
        "const": constants(),
        "nout": chunks(i["norm_out"], KC),
        "par": rows(np.stack(per)), "w1a1": rows(w1a1), "w2a2": rows(w2a2), "rtw": rows(rtw), "s0": rows(s0),
        "ck": rows(i["cache_k"][0].reshape(L, P, KV).transpose(0, 2, 1)),
        "cv": rows(i["cache_v"][0].reshape(L, P, KV)),
        "w_mod": i["w_mod"].reshape(L * D, 6 * D), "w_in": i["w_in"].reshape(L * D, IN_W),
        "w_out": i["w_out"].reshape(L * D, D),
        "exp_w1": i["exp_w1"].reshape(L * N_EXP * D, DE), "exp_w3": i["exp_w3"].reshape(L * N_EXP * D, DE),
        "exp_w2": i["exp_w2"].reshape(L * N_EXP * DE, D),
    }


OUTS = {"yT": (P, KC * T), "kT": (DEPTH * P, TP), "vT": (DEPTH * P, TP), "state": (DEPTH * P, 4 * HD)}


def kernel(**inputs):
    import concourse.bacc as bacc
    from concourse.bass_utils import run_bass_kernel_spmd as run

    nc = bacc.Bacc("TRN2", target_bir_lowering=False, num_devices=1)
    arrays = {f"in_{k}": np.ascontiguousarray(v) for k, v in layouts({k: np.asarray(v) for k, v in inputs.items()}).items()}
    a = {k[3:]: nc.dram_tensor(k, v.shape, F32, kind="ExternalInput").ap() for k, v in arrays.items()}
    o = {k: nc.dram_tensor(f"out_{k}", s, F32, kind="ExternalOutput").ap() for k, s in OUTS.items()}
    build(nc, a, o)
    r = run(nc, [arrays], core_ids=[0]).results[0]
    y = r["out_yT"].reshape(P, KC, T).transpose(2, 1, 0).reshape(T, D)
    k, v = (r[f"out_{n}"].reshape(DEPTH, P, TP).transpose(0, 2, 1).reshape(1, DEPTH, TP, 2, HD) for n in ("kT", "vT"))
    state = r["out_state"].reshape(DEPTH, 2, HD, 2, 2, HD).transpose(0, 3, 4, 1, 5, 2)
    return y[None, :TP].copy(), y[None, TP:].copy(), k.copy(), v.copy(), state.reshape(1, DEPTH, 2, 4, HD, HD).copy()
```
